# Optimizing a Trainium2 kernel written in Bass

```python
import jax, jax.numpy as jnp
from jax import lax
import numpy as np

D_MODEL = 2048
BATCH = 1
SEQ = 256
DEPTH = 1

HEAD_DIM = 128
FOX_HEADS = 8
GDN_HEADS = 8
CONV_CH = 1024
MIX_W = 1024
N_BRANCH = 3
GDN_CONV = 4
CONF_KERNEL = 31
FFN_CONV = 3
D_FF = 5632
MEM_LEN = 256
XA_HEADS = 4
FOX_BLOCK = 128
GDN_CHUNK = 64
FOX_W = FOX_HEADS * HEAD_DIM
GDN_W = GDN_HEADS * HEAD_DIM
XA_W = XA_HEADS * HEAD_DIM
IN_SPLITS = (FOX_W, FOX_W, FOX_W, FOX_HEADS, GDN_W, GDN_W, GDN_W, GDN_HEADS, GDN_HEADS, GDN_W, 2 * CONV_CH, N_BRANCH * D_MODEL)
N_IN = 3 * FOX_W + FOX_HEADS + 4 * GDN_W + 2 * GDN_HEADS + 2 * CONV_CH + N_BRANCH * D_MODEL

kernel_name = "fox_gdn_conformer_parallel_hybrid"

F32 = jnp.float32

def _split(t, sizes):
    idx = np.cumsum(np.array(sizes))[:-1].tolist()
    return jnp.split(t, idx, axis=-1)

def rms_norm(x, g, eps=1e-6):
    xf = x.astype(F32)
    y = xf * lax.rsqrt(jnp.mean(xf * xf, axis=-1, keepdims=True) + eps)
    return (y * g.astype(F32)).astype(x.dtype)

def layer_norm(x, g, b, eps=1e-5):
    xf = x.astype(F32)
    mu = jnp.mean(xf, axis=-1, keepdims=True)
    xc = xf - mu
    y = xc * lax.rsqrt(jnp.mean(xc * xc, axis=-1, keepdims=True) + eps)
    return (y * g.astype(F32) + b.astype(F32)).astype(x.dtype)

def l2_norm(x, eps=1e-6):
    xf = x.astype(F32)
    return xf * lax.rsqrt(jnp.sum(xf * xf, axis=-1, keepdims=True) + eps)

def causal_dwconv(x, w):
    K, C = w.shape
    return lax.conv_general_dilated(
        x, w[:, None, :].astype(x.dtype), window_strides=(1,), padding=((K - 1, 0),),
        dimension_numbers=('NWC', 'WIO', 'NWC'), feature_group_count=C)

def forgetting_attention(q, k, v, log_f):
    B, S, H, D = q.shape
    nb = S // FOX_BLOCK
    F = jnp.cumsum(log_f, axis=1)
    F_k = jnp.transpose(F, (0, 2, 1))
    kf = k.astype(F32)
    vf = v.astype(F32)
    qb = jnp.moveaxis(q.reshape(B, nb, FOX_BLOCK, H, D), 1, 0)
    Fb = jnp.moveaxis(F_k.reshape(B, H, nb, FOX_BLOCK), 2, 0)
    kpos = jnp.arange(S)
    scale = D ** -0.5

    def one_block(args):
        i, q_blk, F_blk = args
        qpos = i * FOX_BLOCK + jnp.arange(FOX_BLOCK)
        s = jnp.einsum('bqhd,bkhd->bhqk', q_blk.astype(F32), kf) * scale
        s = s + F_blk[..., :, None] - F_k[..., None, :]
        s = jnp.where(kpos[None, :] <= qpos[:, None], s, -jnp.inf)
        p = jax.nn.softmax(s, axis=-1)
        return jnp.einsum('bhqk,bkhd->bqhd', p, vf)

    o = lax.map(one_block, (jnp.arange(nb), qb, Fb))
    return jnp.moveaxis(o, 0, 1).reshape(B, S, H, D).astype(v.dtype)

def gated_delta_rule(q, k, v, g, beta):
    B, S, H, dk = q.shape
    dv = v.shape[-1]
    C = GDN_CHUNK
    N = S // C

    def chunk(t):
        return jnp.transpose(t.astype(F32).reshape(B, N, C, H, -1), (0, 3, 1, 2, 4))

    q = chunk(q) * (dk ** -0.5)
    k = chunk(k)
    v = chunk(v)
    g = jnp.transpose(g.astype(F32).reshape(B, N, C, H), (0, 3, 1, 2))
    beta = jnp.transpose(beta.astype(F32).reshape(B, N, C, H), (0, 3, 1, 2))
    g = jnp.cumsum(g, axis=-1)
    causal = jnp.tril(jnp.ones((C, C), dtype=bool))
    strict = jnp.tril(jnp.ones((C, C), dtype=bool), -1)
    decay = jnp.exp(jnp.where(causal, g[..., :, None] - g[..., None, :], -jnp.inf))
    kb = k * beta[..., None]
    vb = v * beta[..., None]
    L = jnp.where(strict, jnp.einsum('bhnid,bhnjd->bhnij', kb, k) * decay, 0.0)
    A = L + jnp.eye(C, dtype=F32)
    rhs = jnp.concatenate([vb, kb * jnp.exp(g)[..., None]], axis=-1)
    sol = lax.linalg.triangular_solve(A, rhs, left_side=True, lower=True, unit_diagonal=True)
    u = sol[..., :dv]
    w = sol[..., dv:]
    attn = jnp.where(causal, jnp.einsum('bhnid,bhnjd->bhnij', q, k) * decay, 0.0)

    def step(state, xs):
        q_i, k_i, u_i, w_i, g_i, a_i = xs
        v_new = u_i - jnp.einsum('bhck,bhkv->bhcv', w_i, state)
        o = jnp.einsum('bhck,bhkv->bhcv', q_i * jnp.exp(g_i)[..., None], state) + jnp.einsum('bhij,bhjv->bhiv', a_i, v_new)
        g_last = g_i[..., -1:]
        state = state * jnp.exp(g_last)[..., None] + jnp.einsum('bhck,bhcv->bhkv', k_i * jnp.exp(g_last - g_i)[..., None], v_new)
        return state, o

    xs = tuple(jnp.moveaxis(t, 2, 0) for t in (q, k, u, w, g, attn))
    state0 = jnp.zeros((B, H, dk, dv), dtype=F32)
    _, o = lax.scan(step, state0, xs)
    return jnp.transpose(o, (1, 0, 3, 2, 4)).reshape(B, S, H, dv)

def hybrid_mixer(h, w_in, fox_fb, fox_q_norm_g, fox_k_norm_g, gdn_conv_w, gdn_a_log, gdn_dt_bias,
                 gdn_out_norm_g, conf_dw_w, conf_dw_b, conf_ln_g, conf_ln_b, w_branch, w_out):
    B, S, _ = h.shape
    p = h @ w_in
    fq, fk, fv, ff, gq, gk, gv, ga, gb, gz, cu, gl = _split(p, IN_SPLITS)
    fq = rms_norm(fq.reshape(B, S, FOX_HEADS, HEAD_DIM), fox_q_norm_g)
    fk = rms_norm(fk.reshape(B, S, FOX_HEADS, HEAD_DIM), fox_k_norm_g)
    fv = fv.reshape(B, S, FOX_HEADS, HEAD_DIM)
    log_f = jax.nn.log_sigmoid(ff.astype(F32) + fox_fb.astype(F32))
    out_a = forgetting_attention(fq, fk, fv, log_f).reshape(B, S, FOX_W)
    qkv = jax.nn.silu(causal_dwconv(jnp.concatenate([gq, gk, gv], axis=-1), gdn_conv_w))
    gq, gk, gv = jnp.split(qkv, [GDN_W, 2 * GDN_W], axis=-1)
    gq = l2_norm(gq.reshape(B, S, GDN_HEADS, HEAD_DIM))
    gk = l2_norm(gk.reshape(B, S, GDN_HEADS, HEAD_DIM))
    gv = gv.reshape(B, S, GDN_HEADS, HEAD_DIM)
    g = -jnp.exp(gdn_a_log.astype(F32)) * jax.nn.softplus(ga.astype(F32) + gdn_dt_bias.astype(F32))
    beta = jax.nn.sigmoid(gb.astype(F32))
    o = gated_delta_rule(gq, gk, gv, g, beta)
    o = rms_norm(o, gdn_out_norm_g) * jax.nn.silu(gz.reshape(B, S, GDN_HEADS, HEAD_DIM).astype(F32))
    out_b = o.reshape(B, S, GDN_W).astype(h.dtype)
    cu_a, cu_g = jnp.split(cu, 2, axis=-1)
    c = cu_a * jax.nn.sigmoid(cu_g)
    c = causal_dwconv(c, conf_dw_w) + conf_dw_b
    out_c = jax.nn.silu(layer_norm(c, conf_ln_g, conf_ln_b))
    branches = jnp.stack([out_a, out_b, out_c], axis=0)
    proj = jnp.einsum('nbsc,ncd->nbsd', branches, w_branch)
    gates = jax.nn.sigmoid(jnp.moveaxis(gl.reshape(B, S, N_BRANCH, D_MODEL), 2, 0).astype(F32))
    y = jnp.sum(gates * proj.astype(F32), axis=0).astype(h.dtype)
    return y @ w_out

def memory_cross_attention(h, m, wq, wkv, q_norm_g, k_norm_g, wo):
    B, S, _ = h.shape
    M = m.shape[1]
    q = rms_norm((h @ wq).reshape(B, S, XA_HEADS, HEAD_DIM), q_norm_g)
    k, v = jnp.split(m @ wkv, 2, axis=-1)
    k = rms_norm(k.reshape(B, M, XA_HEADS, HEAD_DIM), k_norm_g)
    v = v.reshape(B, M, XA_HEADS, HEAD_DIM)
    s = jnp.einsum('bshd,bmhd->bhsm', q.astype(F32), k.astype(F32)) * (HEAD_DIM ** -0.5)
    p = jax.nn.softmax(s, axis=-1)
    o = jnp.einsum('bhsm,bmhd->bshd', p, v.astype(F32)).reshape(B, S, XA_W).astype(h.dtype)
    return o @ wo

def conv_ffn(h, w_up, conv_w, conv_b, w_down):
    a, v = jnp.split(h @ w_up, 2, axis=-1)
    a = causal_dwconv(a, conv_w) + conv_b
    return (jax.nn.silu(a) * v) @ w_down

def setup_inputs(seed: int = 0) -> dict:
    key = jax.random.key(seed)
    ks = jax.random.split(key, 32)

    def nrm(k, shape, scale):
        return jax.random.normal(k, shape, dtype=F32) * scale

    def gain(k, shape):
        return 1.0 + 0.02 * jax.random.normal(k, shape, dtype=F32)

    dt = jnp.exp(jax.random.uniform(ks[8], (DEPTH, GDN_HEADS), minval=float(np.log(1e-3)), maxval=float(np.log(1e-1))))
    return {
        "x": nrm(ks[0], (BATCH, SEQ, D_MODEL), 1.0),
        "mem": nrm(ks[1], (BATCH, MEM_LEN, D_MODEL), 1.0),
        "mix_norm_g": gain(ks[2], (DEPTH, D_MODEL)),
        "w_in": nrm(ks[3], (DEPTH, D_MODEL, N_IN), D_MODEL ** -0.5),
        "fox_fb": jax.random.uniform(ks[4], (DEPTH, FOX_HEADS), minval=0.5, maxval=4.0),
        "fox_q_norm_g": gain(ks[5], (DEPTH, HEAD_DIM)),
        "fox_k_norm_g": gain(ks[6], (DEPTH, HEAD_DIM)),
        "gdn_conv_w": nrm(ks[7], (DEPTH, GDN_CONV, 3 * GDN_W), GDN_CONV ** -0.5),
        "gdn_a_log": jnp.log(jax.random.uniform(ks[9], (DEPTH, GDN_HEADS), minval=1.0, maxval=16.0)),
        "gdn_dt_bias": dt + jnp.log(-jnp.expm1(-dt)),
        "gdn_out_norm_g": gain(ks[10], (DEPTH, HEAD_DIM)),
        "conf_dw_w": nrm(ks[11], (DEPTH, CONF_KERNEL, CONV_CH), CONF_KERNEL ** -0.5),
        "conf_dw_b": nrm(ks[12], (DEPTH, CONV_CH), 0.02),
        "conf_ln_g": gain(ks[13], (DEPTH, CONV_CH)),
        "conf_ln_b": nrm(ks[14], (DEPTH, CONV_CH), 0.02),
        "w_branch": nrm(ks[15], (DEPTH, N_BRANCH, MIX_W, D_MODEL), MIX_W ** -0.5),
        "w_out": nrm(ks[16], (DEPTH, D_MODEL, D_MODEL), D_MODEL ** -0.5),
        "mem_norm_g": gain(ks[17], (D_MODEL,)),
        "xattn_norm_g": gain(ks[18], (DEPTH, D_MODEL)),
        "xattn_wq": nrm(ks[19], (DEPTH, D_MODEL, XA_W), D_MODEL ** -0.5),
        "xattn_wkv": nrm(ks[20], (DEPTH, D_MODEL, 2 * XA_W), D_MODEL ** -0.5),
        "xattn_q_norm_g": gain(ks[21], (DEPTH, HEAD_DIM)),
        "xattn_k_norm_g": gain(ks[22], (DEPTH, HEAD_DIM)),
        "xattn_wo": nrm(ks[23], (DEPTH, XA_W, D_MODEL), XA_W ** -0.5),
        "ffn_norm_g": gain(ks[24], (DEPTH, D_MODEL)),
        "ffn_w_up": nrm(ks[25], (DEPTH, D_MODEL, 2 * D_FF), D_MODEL ** -0.5),
        "ffn_conv_w": nrm(ks[26], (DEPTH, FFN_CONV, D_FF), FFN_CONV ** -0.5),
        "ffn_conv_b": nrm(ks[27], (DEPTH, D_FF), 0.02),
        "ffn_w_down": nrm(ks[28], (DEPTH, D_FF, D_MODEL), D_FF ** -0.5),
    }

def reference(x, mem, mix_norm_g, w_in, fox_fb, fox_q_norm_g, fox_k_norm_g, gdn_conv_w, gdn_a_log,
              gdn_dt_bias, gdn_out_norm_g, conf_dw_w, conf_dw_b, conf_ln_g, conf_ln_b, w_branch, w_out,
              mem_norm_g, xattn_norm_g, xattn_wq, xattn_wkv, xattn_q_norm_g, xattn_k_norm_g, xattn_wo,
              ffn_norm_g, ffn_w_up, ffn_conv_w, ffn_conv_b, ffn_w_down):
    m = rms_norm(mem, mem_norm_g)
    for l in range(DEPTH):
        x = x + hybrid_mixer(rms_norm(x, mix_norm_g[l]), w_in[l], fox_fb[l], fox_q_norm_g[l], fox_k_norm_g[l],
                             gdn_conv_w[l], gdn_a_log[l], gdn_dt_bias[l], gdn_out_norm_g[l], conf_dw_w[l],
                             conf_dw_b[l], conf_ln_g[l], conf_ln_b[l], w_branch[l], w_out[l])
        x = x + memory_cross_attention(rms_norm(x, xattn_norm_g[l]), m, xattn_wq[l], xattn_wkv[l],
                                       xattn_q_norm_g[l], xattn_k_norm_g[l], xattn_wo[l])
        x = x + conv_ffn(rms_norm(x, ffn_norm_g[l]), ffn_w_up[l], ffn_conv_w[l], ffn_conv_b[l], ffn_w_down[l])
    return x


_drawn_inputs = setup_inputs


def setup_inputs(seed=0):
    import zlib

    import numpy as np

    out = dict(_drawn_inputs(seed))
    spreads = {}
    factors = {'mix_norm_g': 3.667,
     'fox_q_norm_g': 8.0,
     'fox_k_norm_g': 8.0,
     'gdn_out_norm_g': 7.966,
     'conf_dw_b': 4.152,
     'conf_ln_g': 18.973,
     'conf_ln_b': 21.506,
     'mem_norm_g': 8.0,
     'xattn_norm_g': 8.0,
     'xattn_q_norm_g': 8.0,
     'xattn_k_norm_g': 8.0,
     'ffn_norm_g': 13.528,
     'ffn_conv_b': 19.027}
    for name, (base, spread) in spreads.items():
        noise = np.random.default_rng([zlib.crc32(name.encode()), seed]).standard_normal(out[name].shape)
        drawn = base * np.exp(spread * noise) if base else spread * noise
        out[name] = __import__('jax').numpy.asarray(drawn.astype(out[name].dtype))
    for name, factor in factors.items():
        out[name] = (out[name] * factor).astype(out[name].dtype)
    return out
```

```python
import numpy as np
import concourse.bass as bass
from concourse import mybir
from contextlib import ExitStack

F32 = mybir.dt.float32
F32R = mybir.dt.float32r
ACT = mybir.ActivationFunctionType
ALU = mybir.AluOpType
AX = mybir.AxisListType

P = 128
T = 256
TT = T // P
D = 2048
DT = D // P
HD = 128
FOX_H = 8
GDN_H = 8
CONV_CH = 1024
CT = CONV_CH // P
BR_T = 1024 // P
GDN_TAPS = 4
CONF_TAPS = 31
FFN_TAPS = 3
D_FF = 5632
FT = D_FF // P
XA_H = 4
CHUNK = 64
NCHUNK = T // CHUNK
EPS = 1e-6
LN_EPS = 1e-5
BIG = -1.0e30

FOX_C = 0
FF_C = 3 * FOX_H * HD
GDN_C = FF_C + FOX_H
GAB_C = GDN_C + 3 * GDN_H * HD
Z_C = GAB_C + 2 * GDN_H
CU_C = Z_C + GDN_H * HD
GL_C = CU_C + 2 * CONV_CH

KS = 2
NC = 512
NT = NC // P
RING = 4
LEAD = 3

PHASES = [("cu", 4, 8), ("gdn", 6, 8), ("fox", 6, 8), ("brC", 4, 12), ("z", 2, 8), ("brA", 4, 12),
          ("brB", 4, 12), ("wout", 4, 8), ("wkv", 2, 8), ("wq", 1, 8), ("wo", 4, 2),
          ("up0", 12, 8), ("down0", 4, 12), ("up1", 10, 8), ("down1", 4, 10)]
BASE = {}
_n = 0
for _name, _g, _s in PHASES:
    BASE[_name] = _n
    _n += _g * _s
SLABS = _n

READ = {}
_n = 0
for _name, _g, _s in PHASES:
    READ[_name] = _n
    _n += _g
GATES = {"brC": 0, "brA": 4, "brB": 8}

def constants():
    t = np.arange(P)
    a, b = t[:, None], t[None, :]
    same = (a // CHUNK) == (b // CHUNK)
    parts = [
        ("upto", (a <= b)),
        ("ones", np.ones((P, P))),
        ("ident", (a == b)),
        ("chunk_upto", (a <= b) & same),
        ("chunk_after", (a > b) & same),
        ("not_before", np.where((a <= b) & same, 0.0, BIG)),
        ("not_strict", np.where((a < b) & same, 0.0, BIG)),
        ("zero", np.zeros((P, P))),
        ("not_causal", np.where(b <= a, 0.0, BIG)),
    ]
    for lv in range(6):
        w = 1 << lv
        m = ((a // (2 * w)) == (b // (2 * w))) & ((b // w) % 2 == 1) & ((a // w) % 2 == 0)
        parts.append((f"level{lv}", m))
    pick = np.zeros((P, 32))
    pick[:, 15] = 1.0
    parts.append(("pick", pick))
    at, off = {}, 0
    for name, m in parts:
        at[name] = (off, off + m.shape[1])
        off += m.shape[1]
    return np.concatenate([m.astype(np.float32) for _, m in parts], axis=1), at


CONST, CONST_AT = constants()

PB = [93, 96, 128, 120, 88, 88]
PO = [sum(PB[:i]) for i in range(len(PB) + 1)]
G_MIX, G_MEM, G_XA, G_FFN = 0, 16, 32, 48
C_DWB, C_LNG, C_LNB = 64, 72, 80
G_FQ, G_FK, G_GO, G_XQ, G_XK = 88, 89, 90, 91, 92
C_GDN = PO[1]
C_CONF = PO[2]
C_FFW = PO[4]
C_FFB = C_FFW + FFN_TAPS * FT

CONV_S, CONV_SLOTS = BASE["gdn"], 96
CONF_S = BASE["brC"]
GDN_N = BASE["fox"]
GDN_S = GDN_N + 9
FOX_N = BASE["fox"] + 34
FOX_V = BASE["brC"] + 6
FOX_S = FOX_V + 1
UNIT_STEPS = 15
HALF_STEPS = 2 * UNIT_STEPS + 7
GDN_STEPS = 2 * HALF_STEPS
FOX_STEPS = 3 * FOX_H
GDN_OUT = BASE["brB"]
MEM_LOAD = [BASE["brB"] + 6, BASE["brB"] + 15]
MEM_S = [BASE["brB"] + 10, BASE["brB"] + 18]
XR_LOAD = [BASE["brB"] + 23, BASE["brB"] + 30]
XR_S = [BASE["brB"] + 26, BASE["brB"] + 33]
Y_SPLIT = BASE["brB"] + 44
NORM2 = BASE["wkv"]
XK_S = BASE["wkv"] + 9
XV_S = BASE["wq"]

NORM_GDN, NORM_FOX, NORM_OUT = (0, 0, 0), (12, 5, 10), (24, 10, 20)
NORM_END = (30, 17, 30)


def gdn_step(slot):
    n = slot - GDN_S
    return n // 2 if n >= 0 and n % 2 == 0 and n // 2 < GDN_STEPS else None


def fox_step(slot):
    n = slot - FOX_S
    return n // 2 if n >= 0 and n % 2 == 0 and n // 2 < FOX_STEPS else None


def gdn_place(step):
    half, n = divmod(step, HALF_STEPS)
    if n < 2 * UNIT_STEPS:
        return half, n // UNIT_STEPS, n % UNIT_STEPS
    return half, None, n - 2 * UNIT_STEPS


ACT_UNIT, ACT_CHAIN = 10, NCHUNK
DVE_UNIT, DVE_CHAIN = 11, 6
ACT_HALF, DVE_HALF = 2 * ACT_UNIT + ACT_CHAIN, 2 * DVE_UNIT + DVE_CHAIN


def chunk_of(n):
    return (0, True) if n == 0 else ((n + 1) // 2, n % 2 == 0)


def gdn_base(half, unit, per_unit, per_half):
    return half * per_half + (2 if unit is None else unit) * per_unit


def dve_chain_base(chunk):
    return (0, 1, 3, 5)[chunk]


def slab_count(n, slot):
    return (n - slot) * (16 // RING) + 16


class Order:

    def __init__(self, eng, sem):
        self.eng, self.sem, self.base, self.n = eng, sem, 0, 0

    def then(self, ins):
        self.n += 1
        ins.then_inc(self.sem, 1)
        self.eng.wait_ge(self.sem, self.base + self.n)

    def enter(self, i, per):
        self.outer, self.per = self.base + self.n, per
        self.base, self.n = self.outer + i * per, 0

    def leave_body(self):
        assert self.n == self.per, (self.n, self.per)

    def leave(self, count):
        self.base, self.n = self.outer + count * self.per, 0


def build(nc, A, out):
    ctx = ExitStack()
    with ctx:
        base = 229376 - nc.sbuf_bytes_remaining
        base = (base + 63) // 64 * 64
        place = [base]

        def sb(name, shape, dt=F32, at=None):
            size = 4
            for s in shape[1:]:
                size *= s
            if at is None:
                at = place[0]
                place[0] += (size + 31) // 32 * 32
            return nc.alloc_sbuf_tensor_at(name, shape, dt, offset=at)

        K = 1024
        cst = sb("cst", [P, CONST.shape[1]])
        par = sb("par", [P, PO[-1]])
        act_hi = sb("act_hi", [P, DT, T], F32R)
        act_lo = sb("act_lo", [P, DT, T], F32R)
        w_f = sb("w_f", [P, RING, KS, NC])
        w_hi = sb("w_hi", [P, RING, KS, NC], F32R)
        w_lo = sb("w_lo", [P, RING, KS, NC], F32R)
        x_at = place[0]
        xres = sb("xres", [P, DT, T])
        eg_b = sb("eg_b", [P, 4, P], at=x_at)
        mt = sb("mt", [P, 4, P], at=x_at + 2 * K)
        lt = sb("lt", [P, 4, P], at=x_at + 4 * K)
        tinv = sb("tinv", [P, 4, P], at=x_at + 6 * K)
        tinv_t = sb("tinv_t", [P, 4, P], at=x_at + 8 * K)
        ys = sb("ys", [P, 4, P], at=x_at + 10 * K)
        state = sb("state", [P, 4, P], at=x_at + 12 * K)
        vnew = sb("vnew", [P, 4, P], at=x_at + 14 * K)
        rg = place[0]
        place[0] += 92 * K
        gdn_all = sb("gdn_all", [P, 3 * GDN_H, T], at=rg)
        gdn_q, gdn_k, gdn_v = (gdn_all[:, i * GDN_H:(i + 1) * GDN_H, :] for i in range(3))
        ob_hi = sb("ob_hi", [P, BR_T, T], F32R, at=rg + 8 * K)
        ob_lo = sb("ob_lo", [P, BR_T, T], F32R, at=rg + 16 * K)
        fox_all = sb("fox_all", [P, 3 * FOX_H, T], at=rg + 24 * K)
        fox_q, fox_k, fox_v = (fox_all[:, i * FOX_H:(i + 1) * FOX_H, :] for i in range(3))
        oa_hi = sb("oa_hi", [P, BR_T, T], F32R, at=rg + 24 * K)
        oa_lo = sb("oa_lo", [P, BR_T, T], F32R, at=rg + 32 * K)
        z_act = sb("z_act", [P, GDN_H, T], at=rg + 40 * K)
        cu_a = sb("cu_a", [P, CT, T], at=rg + 48 * K)
        conf = sb("conf", [P, CT, T], at=rg + 56 * K)
        oc_hi = sb("oc_hi", [P, BR_T, T], F32R, at=rg + 48 * K)
        oc_lo = sb("oc_lo", [P, BR_T, T], F32R, at=rg + 56 * K)
        y = sb("y", [P, DT, T], at=rg + 64 * K)
        attn_t = sb("attn_t", [P, 4, T], at=rg + 80 * K)
        w_t = sb("w_t", [P, 4, T], at=rg + 84 * K)
        gate = sb("gate", [P, NT, T], at=rg + 88 * K)
        x_tok = sb("x_tok", [P, TT, D], at=rg + 64 * K)
        junk = sb("junk", [P, D], at=x_at + 8 * K)
        par_rows = sb("par_rows", [P, len(PB), P], at=rg + 56 * K)
        nar_f = sb("nar_f", [P, DT, 24], at=rg + 80 * K)
        nar_hi = sb("nar_hi", [P, DT, 24], F32R, at=rg + 82 * K)
        nar_lo = sb("nar_lo", [P, DT, 24], F32R, at=rg + 84 * K)
        mem_hi = sb("mem_hi", [P, DT, T], F32R, at=rg + 24 * K)
        mem_lo = sb("mem_lo", [P, DT, T], F32R, at=rg + 48 * K)
        m_tok = sb("m_tok", [P, D], at=rg + 80 * K)
        xr_tok = sb("xr_tok", [P, D], at=rg + 80 * K)
        xo_hi = sb("xo_hi", [P, XA_H, T], F32R, at=rg + 24 * K)
        xo_lo = sb("xo_lo", [P, XA_H, T], F32R, at=rg + 28 * K)
        xa_pt = sb("xa_pt", [P, XA_H, 2 * T], at=rg + 32 * K)
        xa_k = sb("xa_k", [P, XA_H, T], at=rg + 64 * K)
        xa_v = sb("xa_v", [P, XA_H, T], at=rg + 68 * K)
        xa_q = sb("xa_q", [P, XA_H, T], at=rg + 72 * K)
        xa_p = sb("xa_p", [P, XA_H, 2 * T], at=rg + 76 * K)
        HALF_T = 24
        g_hi = sb("g_hi", [P, HALF_T, T], F32R, at=rg)
        g_lo = sb("g_lo", [P, HALF_T, T], F32R, at=rg + 24 * K)
        ff_a = sb("ff_a", [P, NT, T], at=rg + 48 * K)
        ff_t = sb("ff_t", [P, NT, T], at=rg + 52 * K)
        out_tok = sb("out_tok", [P, TT, D], at=rg + 56 * K)
        split_t = sb("split_t", [P, NT, P], at=x_at)
        split_w = sb("split_w", [P, NT, T], at=rg + 88 * K)
        fx_s_at = place[0]
        fx_s = sb("fx_s", [P, 3 * P])
        fx_pt = sb("fx_pt", [P, 3 * P])
        tmp_w = sb("tmp_w", [P, T], at=fx_s_at)
        ms_w = sb("ms_w", [P, T])
        rs_w = sb("rs_w", [P, T])
        ms_t = sb("ms_t", [P, 4])
        rs_t = sb("rs_t", [P, 4])
        tmp_t = sb("tmp_t", [P, 4])
        ssum = sb("ssum", [P, 4])
        xa_m = sb("xa_m", [P, XA_H, 2])
        xa_sum = sb("xa_sum", [P, XA_H, 2])
        nar = sb("nar", [P, TT, 24])
        bias24 = sb("bias24", [P, 24])
        sp_v = sb("sp_v", [P, TT, 24])
        sp_a = sb("sp_a", [P, TT, 24])
        logf_n = sb("logf_n", [P, TT, 8])
        gdn_g = sb("gdn_g", [P, TT, 8])
        ln_beta = sb("ln_beta", [P, TT, 8])
        half_beta = sb("half_beta", [P, TT, 8])
        f_col = sb("f_col", [P, TT, 8])
        g_neg = sb("g_neg", [P, TT, 8])
        beta_eg = sb("beta_eg", [P, TT, 8])
        k_dec = sb("k_dec", [P, TT, 8])
        g_last = sb("g_last", [P, GDN_H, NCHUNK])
        fx_m = sb("fx_m", [P, 2])
        fx_sum = sb("fx_sum", [P, 2])
        qgain = sb("qgain", [P, 2])
        assert place[0] <= 229376, place[0]

        ps = [ctx.enter_context(nc.psum_tensor(f"ps{i}", [P, NT, T], F32)) for i in range(2)]
        bk = [ctx.enter_context(nc.psum_tensor(f"bk{i}", [P, 512], F32)) for i in range(4)]
        FA, FB, GA, GB = bk

        def sem(name):
            return ctx.enter_context(nc.semaphore(name))

        slab_loaded = [sem(f"slab_loaded{i}") for i in range(RING)]
        slab_hi, slab_lo, slab_used = sem("slab_hi"), sem("slab_lo"), sem("slab_used")
        group_read = sem("group_read")
        gates_read = sem("gates_read")
        const_in, param_in, nar_in, bias_in = sem("const_in"), sem("param_in"), sem("nar_in"), sem("bias_in")
        x_in = [sem(f"x_in{t}") for t in range(TT)]
        mem_in = [sem(f"mem_in{t}") for t in range(TT)]
        xr_in = [sem(f"xr_in{t}") for t in range(TT)]
        out_st = sem("out_st")
        act_own, dve_own = sem("act_own"), sem("dve_own")
        pre_pe, pre_act, pre_dve = sem("pre_pe"), sem("pre_act"), sem("pre_dve")
        h_ready = sem("h_ready")
        silu_done = sem("silu_done")
        tanh_out = sem("tanh_out")
        y_added = sem("y_added")
        nm_pe, nm_act, nm_dve = sem("nm_pe"), sem("nm_act"), sem("nm_dve")
        cf_pe, cf_act, cf_dve = sem("cf_pe"), sem("cf_act"), sem("cf_dve")
        fx_pe, fx_act, fx_dve = sem("fx_pe"), sem("fx_act"), sem("fx_dve")
        gd_pe, gd_act, gd_dve = sem("gd_pe"), sem("gd_act"), sem("gd_dve")
        mm_pe, mm_act, mm_dve = sem("mm_pe"), sem("mm_act"), sem("mm_dve")
        xr_pe, xr_act = sem("xr_pe"), sem("xr_act")
        y_act, y_ready = sem("y_act"), sem("y_ready")
        mn_pe, mn_act, mn_dve = sem("mn_pe"), sem("mn_act"), sem("mn_dve")
        xa_pe, xa_act, xa_dve = sem("xa_pe"), sem("xa_act"), sem("xa_dve")
        ff_act, g_ready = sem("ff_act"), sem("g_ready")
        fin_pe, fin_act = sem("fin_pe"), sem("fin_act")

        def c(name, rows=slice(None)):
            a, b = CONST_AT[name]
            return cst[rows, a:b]

        def col(i):
            return par[:, i:i + 1]

        upto, ones, ident = c("upto"), c("ones"), c("ident")
        upto_ones = cst[:, CONST_AT["upto"][0]:CONST_AT["ones"][1]]
        zero_causal = cst[:, CONST_AT["zero"][0]:CONST_AT["not_causal"][1]]
        chunk_upto, chunk_after = c("chunk_upto"), c("chunk_after")

        def over(ap, n):
            return ap.unsqueeze(1).to_broadcast([ap.shape[0], n, ap.shape[1]])

        def spread(column, n=P):
            return column.to_broadcast([column.shape[0], n])

        def pick(i):
            o = CONST_AT["pick"][0]
            return cst[:, o + 15 - i:o + 31 - i]

        w_in, w_br, w_out = A["w_in"][0], A["w_branch"][0], A["w_out"][0]
        wq, wkv, wo = A["xattn_wq"][0], A["xattn_wkv"][0], A["xattn_wo"][0]
        w_up, w_down = A["ffn_w_up"][0], A["ffn_w_down"][0]

        block = ctx.enter_context(nc.Block())

        @block.sync
        def _(sp):
            sp.dma_start(x_tok[:, 0, :], A["x"][0, 0:P, :]).then_inc(x_in[0], 16)
            sp.dma_start(cst[:, :], A["const"]).then_inc(const_in, 16)
            row = [0]

            def rows(blk, src):
                n = src.shape[0]
                sp.dma_start(par_rows[row[0]:row[0] + n, blk, :], src).then_inc(param_in, 16)
                row[0] += n

            for name in ("mix_norm_g", "mem_norm_g", "xattn_norm_g", "ffn_norm_g", "conf_dw_b", "conf_ln_g", "conf_ln_b"):
                v = A[name] if name == "mem_norm_g" else A[name][0]
                rows(0, v.rearrange("(r c) -> r c", c=P))
            for name in ("fox_q_norm_g", "fox_k_norm_g", "gdn_out_norm_g", "xattn_q_norm_g", "xattn_k_norm_g"):
                rows(0, A[name])
            row[0] = 0
            rows(1, A["gdn_conv_w"][0].rearrange("k (t c) -> (k t) c", c=P))
            row[0] = 0
            dw = A["conf_dw_w"][0].rearrange("k (t c) -> (k t) c", c=P)
            rows(2, dw[0:P, :])
            row[0] = 0
            rows(3, dw[P:CONF_TAPS * CT, :])
            row[0] = 0
            fw = A["ffn_conv_w"][0].rearrange("k (t c) -> (k t) c", c=P)
            rows(4, fw[0:2 * FT, :])
            row[0] = 0
            rows(5, fw[2 * FT:3 * FT, :])
            rows(5, A["ffn_conv_b"][0].rearrange("(r c) -> r c", c=P))
            sp.dma_start(x_tok[:, 1, :], A["x"][0, P:T, :]).then_inc(x_in[1], 16)
            for j, name in enumerate(("fox_fb", "gdn_dt_bias", "gdn_a_log")):
                sp.dma_start(bias24[:, 8 * j:8 * j + 8], A[name].to_broadcast([P, 8])).then_inc(bias_in, 16)
            w3 = w_in.rearrange("(a p) n -> p a n", p=P)
            sp.dma_start(nar_f[:, :, 0:8], w3[:, :, FF_C:FF_C + 8]).then_inc(nar_in, 16)
            sp.dma_start(nar_f[:, :, 8:24], w3[:, :, GAB_C:GAB_C + 16]).then_inc(nar_in, 16)

            def group(n0, w, k_slabs, g, c0, slot0=0, first=0):
                for j in range(k_slabs):
                    n, slot = n0 + j, (slot0 + j) % RING
                    if not isinstance(n, int) or n >= RING:
                        sp.wait_ge(slab_lo, n - (RING - 1))
                    r = (first + j) * KS * P
                    src = w[r:r + KS * P, bass.ds(g * NC + c0, NC)].rearrange("(a p) n -> p a n", p=P)
                    sp.dma_start(w_f[:, slot, :, :], src).then_inc(slab_loaded[slot], 16)

            group(0, w_in, 8, 0, CU_C)
            with sp.Fori(1, 4) as g:
                group(g * 8, w_in, 8, g, CU_C)
            for name, count, c0 in (("gdn", 6, GDN_C), ("fox", 6, FOX_C)):
                with sp.Fori(0, count) as g:
                    group(g * 8 + BASE[name], w_in, 8, g, c0)
            for n, name in ((2, "brC"), (0, "brA"), (1, "brB")):
                with sp.Fori(1, 5) as g:
                    group(g * 12 + (BASE[name] - 12), w_in, 8, g, GL_C + n * D - NC)
                    group(g * 12 + (BASE[name] - 4), w_br[n], 4, g, -NC)
                if name == "brC":
                    with sp.Fori(0, 2) as g:
                        group(g * 8 + BASE["z"], w_in, 8, g, Z_C)
            with sp.Fori(0, 4) as g:
                group(g * 8 + BASE["wout"], w_out, 8, g, 0)
            with sp.Fori(0, 2) as g:
                group(g * 8 + BASE["wkv"], wkv, 8, g, 0)
            group(BASE["wq"], wq, 8, 0, 0)
            for g in range(4):
                group(BASE["wo"] + 2 * g, wo, 2, g, 0, slot0=2 * g)
            for half, (a, pairs) in enumerate(((0, 6), (6, 5))):
                with sp.Fori(0, pairs) as g:
                    group(g * 16 + BASE[f"up{half}"], w_up, 8, g, a * NC)
                    group(g * 16 + (BASE[f"up{half}"] + 8), w_up, 8, g, a * NC + D_FF)
                per = 12 - 2 * half
                with sp.Fori(0, 2) as g2:
                    for k in range(2):
                        group(g2 * (2 * per) + (BASE[f"down{half}"] + k * per), w_down, per, g2 * 2, k * NC,
                              slot0=k * per, first=12 * half)
            sp.wait_ge(fin_act, 8)
            for t in range(TT):
                sp.dma_start(out[0, t * P:(t + 1) * P, :], out_tok[:, t, :]).then_inc(out_st, 16)
            sp.wait_ge(out_st, 16 * TT)

        @block.tensor
        def _(pe):
            mm = nc.tensor.matmul
            transpose = nc.tensor.transpose

            def slab(n, slot, psum, hi, lo, k0, first, last):
                pe.wait_ge(slab_lo, n + 1)
                for kk in range(KS):
                    for j in range(NT):
                        wh = w_hi[:, slot, kk, j * P:(j + 1) * P]
                        wl = w_lo[:, slot, kk, j * P:(j + 1) * P]
                        o = psum[:, j, :]
                        mm(o, wh, hi[:, k0 + kk, :], start=first and kk == 0 and j % 2 == 0, stop=False, skip_group_check=True)
                        mm(o, wh, lo[:, k0 + kk, :], start=False, stop=False, skip_group_check=True)
                        i = mm(o, wl, hi[:, k0 + kk, :], start=False, stop=last and kk == KS - 1, skip_group_check=True)
                i.then_inc(slab_used, 1)

            def group(n0, buf, hi, lo, k_slabs, slot0=0, slots=None, ready=None):
                for j in range(k_slabs):
                    if ready is not None:
                        pe.wait_ge(ready[0], ready[1](j))
                    slab(n0 + j, (slot0 + j) % RING, ps[buf], hi, lo, KS * j, j == 0, j == k_slabs - 1)
                    if slots is not None:
                        slots(n0 + j)

            pe.wait_ge(const_in, 16)
            pe.wait_ge(param_in, 16 * 18)
            for b, n in enumerate(PB):
                transpose(bk[b // 3][:, (b % 3) * P:(b % 3) * P + n], par_rows[0:n, b, :], ident[0:n, 0:n])\
                    .then_inc(pre_pe, 1)
            for b in range(8):
                t, k = divmod(b, 4)
                pe.wait_ge(pre_dve, 3 + 2 * t)
                if b >= 2:
                    pe.wait_ge(pre_dve, 4 + b)
                for j in range(4):
                    i = transpose(bk[2 + b % 2][:, j * P:(j + 1) * P], x_tok[:, t, (4 * k + j) * P:(4 * k + j + 1) * P], ident)
                i.then_inc(pre_pe, 1)
            pe.wait_ge(h_ready, 8)
            pe.wait_ge(pre_dve, 14)
            for t in range(TT):
                o = FA[:, t * 24:t * 24 + 24]
                for k in range(DT):
                    ah, al = act_hi[:, k, t * P:(t + 1) * P], act_lo[:, k, t * P:(t + 1) * P]
                    mm(o, ah, nar_hi[:, k, :], start=(t == 0 and k == 0), stop=False, skip_group_check=True)
                    mm(o, ah, nar_lo[:, k, :], start=False, stop=False, skip_group_check=True)
                    i = mm(o, al, nar_hi[:, k, :], start=False, stop=(k == DT - 1), skip_group_check=True)
            i.then_inc(pre_pe, 1)

            def token_sums():
                pe.wait_ge(pre_dve, 16)
                mm(FB[:, 0:8], upto, logf_n[:, 0, :], start=True, stop=True)
                mm(FB[:, 8:16], ones, logf_n[:, 0, :], start=True, stop=False)
                mm(FB[:, 8:16], upto, logf_n[:, 1, :], start=False, stop=True)
                for t in range(TT):
                    mm(FB[:, 16 + 8 * t:24 + 8 * t], chunk_upto, gdn_g[:, t, :], start=True, stop=True)
                    i = mm(FB[:, 32 + 8 * t:40 + 8 * t], chunk_after, gdn_g[:, t, :], start=True, stop=True)
                i.then_inc(pre_pe, 1)

            def head_norm(n, events, acc, banks, tiles, per_pair=1):
                _, a0, d0 = events
                nb = tiles // 4
                if n < nb:
                    pe.wait_ge(nm_act, a0 + n + 1)
                    for j in range(4):
                        i = mm(acc[0:16, 0:T], pick(4 * n + j), gate[:, j, :], start=(n == 0 and j == 0),
                               stop=(n == nb - 1 and j == 3))
                    i.then_inc(nm_pe, 1)
                    return
                for pr in (2 * (n - nb), 2 * (n - nb) + 1):
                    pe.wait_ge(nm_dve, d0 + 2 + (per_pair * (pr - 2) + 1 if pr >= 2 else 0))
                    for j in range(2):
                        i = mm(banks[pr % 2][:, j * T:(j + 1) * T], spread(ident[0:16, 2 * pr + j:2 * pr + j + 1]), rs_w[0:16, :],
                               start=(j == 0), stop=True, skip_group_check=True)
                    i.then_inc(nm_pe, 1)

            def fox_v_by_token():
                pe.wait_ge(cf_dve, 3)
                pe.wait_ge(nm_dve, NORM_OUT[2])
                for b in range(4):
                    if b >= 2:
                        pe.wait_ge(fx_act, b - 1)
                    for j in range(4):
                        h, t = 2 * b + j // 2, j % 2
                        i = transpose((FA, FB)[b % 2][:, j * P:(j + 1) * P], fox_v[:, h, t * P:(t + 1) * P], ident)
                    i.then_inc(fx_pe, 1)

            def fox(step):
                h, s = divmod(step, 3)
                if s == 0:
                    pe.wait_ge(fx_act, 4 + 3 * h)
                    if h:
                        pe.wait_ge(fx_dve, 3 * h)
                    q, k = fox_q[:, h, :], fox_k[:, h, :]
                    mm(FA[:, 0:P], q[:, 0:P], k[:, 0:P], start=True, stop=False, skip_group_check=True)
                    mm(FA[:, P:3 * P], q[:, P:T], k, start=False, stop=False, skip_group_check=True)
                    f0, f1 = spread(logf_n[:, 0, h:h + 1]), spread(logf_n[:, 1, h:h + 1])
                    mm(FA[:, 0:P], f0, upto, start=False, stop=True, skip_group_check=True)
                    mm(FA[:, P:3 * P], f0, upto_ones, start=False, stop=False, skip_group_check=True)
                    i = mm(FA[:, 2 * P:3 * P], f1, upto, start=False, stop=True, skip_group_check=True)
                elif s == 1:
                    pe.wait_ge(fx_dve, 3 * h + 2)
                    for j in range(3):
                        i = transpose(FB[:, j * P:(j + 1) * P], fx_s[:, j * P:(j + 1) * P], ident)
                else:
                    pe.wait_ge(fx_act, 4 + 3 * h + 2)
                    v = fox_v[:, h, :]
                    mm(FA[:, 0:T], v[:, 0:P], fx_pt[:, 0:T], start=True, stop=False, skip_group_check=True)
                    i = mm(FA[:, P:T], v[:, P:T], fx_pt[:, T:3 * P], start=False, stop=True, skip_group_check=True)
                i.then_inc(fx_pe, 1)

            def gdn(step):
                half, unit, s = gdn_place(step)
                a0 = gdn_base(half, unit, ACT_UNIT, ACT_HALF)
                d0 = gdn_base(half, unit, DVE_UNIT, DVE_HALF)
                if unit is None:
                    gdn_chain(half, s, a0, d0)
                    return
                mats = [(2 * i + p, 4 * half + 2 * unit + i, p) for i in range(2) for p in range(2)]

                def tok(m, h, p):
                    return m[:, h, p * P:(p + 1) * P]

                def o(bank, m):
                    return bank[:, m * P:(m + 1) * P]

                if s == 0:
                    if step:
                        pe.wait_ge(gd_act, a0)
                        pe.wait_ge(gd_dve, d0)
                    else:
                        pe.wait_ge(nm_dve, NORM_FOX[2])
                    for m, h, p in mats:
                        mm(o(GA, m), spread(gdn_g[:, p, h:h + 1]), chunk_upto, start=(m == 0), stop=False, skip_group_check=True)
                    for m, h, p in mats:
                        i = mm(o(GB, m), tok(gdn_k, h, p), tok(gdn_q, h, p), start=True, stop=True)
                elif s == 1:
                    pe.wait_ge(gd_dve, d0 + 2)
                    for m, h, p in mats:
                        mm(o(GA, m), spread(ln_beta[:, p, h:h + 1]), ident, start=False, stop=True, skip_group_check=True)
                    for m, h, p in mats:
                        i = mm(o(GB, m), tok(gdn_k, h, p), tok(gdn_k, h, p), start=True, stop=True)
                elif s == 2:
                    pe.wait_ge(gd_dve, d0 + 4)
                    for m, h, p in mats:
                        i = transpose(o(GA, m), mt[:, m, :], ident)
                elif s < 13:
                    lv, second = (s - 1) // 2, (s - 3) % 2
                    if not second:
                        pe.wait_ge(gd_dve, d0 + 4 + lv)
                        for m, h, p in mats:
                            i = mm(o(GA, m), mt[:, m, :], tinv[:, m, :], start=True, stop=True)
                    else:
                        pe.wait_ge(gd_act, a0 + 3 + lv)
                        if lv < 5:
                            for m, h, p in mats:
                                mm(o(GB, m), tinv_t[:, m, :], ys[:, m, :], start=True, stop=True)
                        for m, h, p in mats:
                            i = mm(o(GA, m), ys[:, m, :], tinv_t[:, m, :], start=True, stop=True)
                elif s == 13:
                    pe.wait_ge(gd_dve, d0 + 10)
                    for m, h, p in mats:
                        transpose(o(GB, m), tok(gdn_k, h, p), ident)
                    for m, h, p in mats:
                        i = transpose(o(GA, m), tok(gdn_v, h, p), ident)
                else:
                    pe.wait_ge(gd_dve, d0 + 11)
                    pe.wait_ge(gd_act, a0 + 9)
                    for m, h, p in mats:
                        mm(o(GA, m), tinv_t[:, m, :], mt[:, m, :], start=True, stop=True)
                    for m, h, p in mats:
                        i = mm(o(GB, m), ys[:, m, :], tinv_t[:, m, :], start=True, stop=True)
                i.then_inc(gd_pe, 1)

            def gdn_chain(half, s, a0, d0):
                ch, second = chunk_of(s)
                p, r = ch // 2, slice((ch % 2) * CHUNK, (ch % 2 + 1) * CHUNK)
                tok = slice(ch * CHUNK, (ch + 1) * CHUNK)
                dc = d0 + dve_chain_base(ch)
                if not second:
                    pe.wait_ge(gd_dve, dc)
                    for i4 in range(4):
                        i = mm(GA[r, i4 * P:(i4 + 1) * P], w_t[:, i4, tok], state[:, i4, :], start=True, stop=True)
                    i.then_inc(gd_pe, 1)
                    return
                pe.wait_ge(gd_act, a0 + ch)
                pe.wait_ge(gd_dve, dc + 1 if ch else d0)
                for i4 in range(4):
                    h = 4 * half + i4
                    vn = vnew[r, i4, :] if ch else gdn_v[r, h, 0:P]
                    o = GB[:, i4 * CHUNK:(i4 + 1) * CHUNK]
                    if ch:
                        mm(o, state[:, i4, :], gdn_q[:, h, tok], start=True, stop=False)
                    i = mm(o, vn, attn_t[r, i4, tok], start=(ch == 0), stop=True)
                if ch < NCHUNK - 1:
                    for i4 in range(4):
                        h = 4 * half + i4
                        vn = vnew[r, i4, :] if ch else gdn_v[r, h, 0:P]
                        i = mm(GA[:, i4 * P:(i4 + 1) * P], gdn_k[r, h, p * P:(p + 1) * P], vn, start=True, stop=True)
                i.then_inc(gd_pe, 1)

            def conf_ln(n):
                if n == 0:
                    pe.wait_ge(nm_dve, NORM_OUT[2])
                    pe.wait_ge(cf_act, 1)
                    for k in range(CT):
                        i = mm(FA[:, 0:T], ones, conf[:, k, :], start=(k == 0), stop=(k == CT - 1))
                else:
                    pe.wait_ge(cf_act, 1 + n)
                    for k in range(4):
                        i = mm(FA[:, T:2 * T], ones, gate[:, k, :], start=(n == 1 and k == 0), stop=(n == 2 and k == 3))
                i.then_inc(cf_pe, 1)

            def mem_batch(t, k):
                b = 4 * t + k
                pe.wait_ge(mm_dve, 10 * t + 2 + 2 * k)
                for j in range(4):
                    i = transpose(FA[:, j * P:(j + 1) * P], m_tok[:, (4 * k + j) * P:(4 * k + j + 1) * P], ident)
                i.then_inc(mm_pe, 1)

            def xr_batch(t, k):
                b = 4 * t + k
                pe.wait_ge(xr_in[t], 16)
                if b >= 2:
                    pe.wait_ge(xr_act, b - 1)
                else:
                    pe.wait_ge(mm_dve, 20)
                for j in range(4):
                    i = transpose((FA, FB)[b % 2][:, j * P:(j + 1) * P], xr_tok[:, (4 * k + j) * P:(4 * k + j + 1) * P], ident)
                i.then_inc(xr_pe, 1)

            def slots(s):
                if s == 0:
                    token_sums()
                if 0 <= s - GDN_N < 8:
                    head_norm(s - GDN_N, NORM_GDN, GA, (GA, GB), 16)
                if 0 <= s - FOX_N < 8:
                    head_norm(s - FOX_N, NORM_FOX, FA, (FA, FB), 16)
                if 0 <= s - CONF_S < 3:
                    conf_ln(s - CONF_S)
                if s == FOX_V:
                    fox_v_by_token()
                if fox_step(s) is not None:
                    fox(fox_step(s))
                if gdn_step(s) is not None:
                    gdn(gdn_step(s))
                if 0 <= s - GDN_OUT < 4:
                    if s == GDN_OUT:
                        pe.wait_ge(gd_act, 2 * ACT_HALF)
                        pe.wait_ge(gd_dve, 2 * DVE_HALF)
                    head_norm(s - GDN_OUT, NORM_OUT, GA, (GA, GB), 8, per_pair=2)
                for t in range(TT):
                    if 1 <= s - MEM_S[t] < 5:
                        mem_batch(t, s - MEM_S[t] - 1)
                    if 0 <= s - XR_S[t] < 4:
                        xr_batch(t, s - XR_S[t])

            def even(name, i, hi, lo, k_slabs, slots=None):
                r = READ[name] + i
                if r >= 2:
                    pe.wait_ge(group_read, r - 1)
                group(BASE[name] + i * k_slabs, i % 2, hi, lo, k_slabs, slot0=i * k_slabs, slots=slots)

            def branch(name, hi, lo, ready, last_gate):
                for g in range(4):
                    n0, gr = BASE[name] + 12 * g, GATES[name] + g
                    if g or last_gate:
                        pe.wait_ge(gates_read, gr)
                    else:
                        pe.wait_ge(group_read, READ[name] - 1)
                    group(n0, 0, act_hi, act_lo, 8, slots=slots)
                    pe.wait_ge(group_read, READ[name] + g)
                    if g == 0:
                        ready()
                    group(n0 + 8, 1, hi, lo, 4, slots=slots)

            for i in range(4):
                even("cu", i, act_hi, act_lo, 8, slots)
            with pe.Fori(0, 3) as g:
                for k in range(2):
                    pe.wait_ge(group_read, g * 2 + (READ["gdn"] + k - 1))
                    group(g * 16 + (BASE["gdn"] + 8 * k), k, act_hi, act_lo, 8)
            for i in range(6):
                even("fox", i, act_hi, act_lo, 8, slots)

            def conf_ready():
                pe.wait_ge(cf_dve, 8)

            def fox_ready():
                pe.wait_ge(fx_dve, 3 * FOX_H)

            def gdn_ready():
                pe.wait_ge(nm_dve, NORM_END[2])

            branch("brC", oc_hi, oc_lo, conf_ready, False)
            pe.wait_ge(gates_read, 4)
            for i in range(2):
                even("z", i, act_hi, act_lo, 8, slots)
            branch("brA", oa_hi, oa_lo, fox_ready, False)
            branch("brB", ob_hi, ob_lo, gdn_ready, True)

            pe.wait_ge(gates_read, 12)
            pe.wait_ge(y_ready, 4)
            with pe.Fori(0, 2) as g:
                for k in range(2):
                    pe.wait_ge(group_read, g * 2 + (READ["wout"] + k - 1))
                    group(g * 16 + (BASE["wout"] + 8 * k), k, act_hi, act_lo, 8)

            def x_norm_sums(m, b):
                pe.wait_ge(mn_act, 9 * m + b + 1)
                for j in range(4):
                    i = mm(FA[:, 0:T], ones, split_w[:, j, :], start=(b == 0 and j == 0), stop=(b == 3 and j == 3))
                i.then_inc(mn_pe, 1)

            def xa_sums(src_events):
                a, = src_events
                pe.wait_ge(xa_act, a)
                for j in range(4):
                    i = mm(FA[0:16, 0:T], pick(j), gate[:, j, :], start=(j == 0), stop=(j == 3))
                i.then_inc(xa_pe, 1)

            def xa_rms(d):
                pe.wait_ge(xa_dve, d)
                for pr in range(2):
                    for j in range(2):
                        i = mm((FA, FB)[pr][:, j * T:(j + 1) * T], spread(ident[0:16, 2 * pr + j:2 * pr + j + 1]), rs_w[0:16, :],
                               start=(j == 0), stop=True, skip_group_check=True)
                    i.then_inc(xa_pe, 1)

            def late(s):
                if 0 <= s - NORM2 < 4:
                    x_norm_sums(0, s - NORM2)
                if s == XK_S:
                    xa_sums((1,))
                if s == XK_S + 1:
                    xa_rms(2)
                if s == XV_S:
                    pe.wait_ge(group_read, READ["wkv"] + 2)
                    for h in range(XA_H):
                        for t in range(TT):
                            i = transpose((GA, GB)[h // 2][:, (h % 2) * T + t * P:(h % 2) * T + (t + 1) * P],
                                          xa_v[:, h, t * P:(t + 1) * P], ident)
                    i.then_inc(xa_pe, 1)

            for i in range(2):
                even("wkv", i, mem_hi, mem_lo, 8, late)
            pe.wait_ge(mn_dve, 10)
            even("wq", 0, act_hi, act_lo, 8, late)
            xa_sums((4,))
            xa_rms(6)
            pe.wait_ge(xa_dve, 8)
            pe.wait_ge(xa_act, 5)
            for h in range(XA_H):
                for t in range(TT):
                    i = mm(bk[h][:, t * T:(t + 1) * T], xa_q[:, h, t * P:(t + 1) * P], xa_k[:, h, :], start=True, stop=True)
                i.then_inc(xa_pe, 1)
            for h in range(XA_H):
                pe.wait_ge(xa_dve, 13 + h)
                for t in range(TT):
                    for m in range(2):
                        i = transpose(bk[h][:, m * T + t * P:m * T + (t + 1) * P], xa_p[:, h, t * T + m * P:t * T + (m + 1) * P], ident)
                i.then_inc(xa_pe, 1)
            for h in range(XA_H):
                pe.wait_ge(xa_act, 10 + h)
                for m in range(2):
                    i = mm(bk[h][:, 0:T], xa_v[:, h, m * P:(m + 1) * P], xa_pt[:, h, m * T:(m + 1) * T], start=(m == 0), stop=(m == 1))
                i.then_inc(xa_pe, 1)
            pe.wait_ge(xa_dve, 20)
            for i in range(4):
                pe.wait_ge(group_read, READ["wo"] + i - (i > 0))
                group(BASE["wo"] + 2 * i, i % 2, xo_hi, xo_lo, 2, slot0=2 * i)
            for b in range(4):
                x_norm_sums(1, b)
            pe.wait_ge(mn_dve, 20)

            done = 0
            for half, pairs in enumerate((6, 5)):
                r = READ[f"up{half}"]
                with pe.Fori(0, pairs) as g:
                    for k in range(2):
                        pe.wait_ge(group_read, g * 2 + (r + k - 1))
                        group(g * 16 + (BASE[f"up{half}"] + 8 * k), k, act_hi, act_lo, 8)
                per, r = 12 - 2 * half, READ[f"down{half}"]
                with pe.Fori(0, 2) as g:
                    for k in range(2):
                        pe.wait_ge(group_read, g * 2 + (r + k - 1))
                        group(g * (2 * per) + (BASE[f"down{half}"] + k * per), k, g_hi, g_lo, per, slot0=k * per,
                              ready=(g_ready, lambda j: done + j // 2 + 1))
                done += pairs
            for b in range(8):
                g, t = divmod(b, 2)
                pe.wait_ge(group_read, READ["down1"] + g + 1)
                if b >= 4:
                    pe.wait_ge(fin_act, b - 3)
                for j in range(4):
                    i = transpose(bk[b % 4][:, j * P:(j + 1) * P], xres[:, 4 * g + j, t * P:(t + 1) * P], ident)
                i.then_inc(fin_pe, 1)

        @block.scalar
        def _(act):
            own = Order(act, act_own)
            op = nc.scalar.activation

            def split(n, slot):
                act.wait_ge(slab_loaded[slot], slab_count(n, slot))
                if not isinstance(n, int) or n >= RING:
                    act.wait_ge(slab_used, n - (RING - 1))
                op(w_hi[:, slot, :, :], w_f[:, slot, :, :], ACT.Copy).then_inc(slab_hi, 1)

            def rsqrt(dst, src):
                own.then(op(dst, src, ACT.Ln))
                return op(dst, dst, ACT.Exp, scale=-0.5)

            for t in range(TT):
                act.wait_ge(x_in[t], 16)
                if t:
                    act.wait_ge(pre_act, 1)
                op(junk[:, :], x_tok[:, t, :], ACT.Square, accum_out=ssum[:, t:t + 1]).then_inc(pre_act, 1)
                act.wait_ge(pre_dve, 2 + 2 * t)
                rsqrt(rs_t[:, t:t + 1], ms_t[:, t:t + 1]).then_inc(pre_act, 1)
            for n in range(LEAD):
                split(n, n)
            for b in range(8):
                t, k = divmod(b, 4)
                act.wait_ge(pre_dve, 6 + b)
                op(act_hi[:, 4 * k:4 * k + 4, t * P:(t + 1) * P], split_t[:, :, :], ACT.Copy).then_inc(pre_act, 1)
            act.wait_ge(nar_in, 32)
            op(nar_hi[:, :, :], nar_f[:, :, :], ACT.Copy).then_inc(pre_act, 1)
            act.wait_ge(bias_in, 48)
            own.then(op(bias24[:, 16:24], bias24[:, 16:24], ACT.Exp))
            act.wait_ge(pre_dve, 15)
            own.then(op(sp_a[:, :, :], sp_v[:, :, :], ACT.Abs))
            own.then(op(sp_a[:, :, :], sp_a[:, :, :], ACT.Exp, scale=-1.0))
            op(sp_a[:, :, :], sp_a[:, :, :], ACT.Ln, bias=1.0).then_inc(pre_act, 1)

            def token_exps():
                act.wait_ge(pre_dve, 16)
                op(half_beta[:, :, :], ln_beta[:, :, :], ACT.Exp).then_inc(pre_act, 1)
                act.wait_ge(pre_dve, 17)
                op(k_dec[:, :, :], FB[:, 32:48], ACT.Exp)
                op(beta_eg[:, :, :], beta_eg[:, :, :], ACT.Exp).then_inc(pre_act, 1)

            def head_norm(n, events, region, tiles):
                p0, a0, d0 = events
                nb = tiles // 4
                if n < nb:
                    if n:
                        act.wait_ge(nm_pe, p0 + n)
                    op(gate[:, :, :], region[:, 4 * n:4 * n + 4, :], ACT.Square).then_inc(nm_act, 1)
                elif n == nb:
                    act.wait_ge(nm_dve, d0 + 1)
                    rsqrt(rs_w[0:16, :], ms_w[0:16, :]).then_inc(nm_act, 1)

            def conf_ln(n):
                if n == 0:
                    act.wait_ge(cf_dve, 1)
                    for k in range(CT):
                        i = op(conf[:, k, :], conf[:, k, :], ACT.Identity, scale=0.5, bias=col(C_DWB + k))
                    i.then_inc(cf_act, 1)
                elif n < 3:
                    act.wait_ge(cf_dve, 2)
                    if n == 1:
                        act.wait_ge(nm_dve, NORM_OUT[2])
                    if n == 2:
                        act.wait_ge(cf_pe, 2)
                    op(gate[:, :, :], conf[:, 4 * n - 4:4 * n, :], ACT.Square).then_inc(cf_act, 1)
                elif n == 3:
                    act.wait_ge(cf_dve, 3)
                    rsqrt(rs_w[:, :], ms_w[:, :]).then_inc(cf_act, 1)
                    act.wait_ge(cf_dve, 4)
                    for k in range(CT):
                        i = op(conf[:, k, :], conf[:, k, :], ACT.Identity, scale=col(C_LNG + k), bias=col(C_LNB + k))
                    i.then_inc(cf_act, 1)
                    act.wait_ge(cf_act, 5)
                    for hf in range(2):
                        if hf:
                            act.wait_ge(cf_dve, 5)
                        op(gate[:, :, :], conf[:, 4 * hf:4 * hf + 4, :], ACT.Tanh, scale=0.5).then_inc(cf_act, 1)
                        act.wait_ge(cf_dve, 5 + 2 * hf)
                        op(oc_hi[:, 4 * hf:4 * hf + 4, :], conf[:, 4 * hf:4 * hf + 4, :], ACT.Copy, scale=0.5).then_inc(cf_act, 1)

            def fox_v_by_token():
                for b in range(4):
                    act.wait_ge(fx_pe, b + 1)
                    op(fox_v[:, 2 * b:2 * b + 2, :], (FA, FB)[b % 2][:, :], ACT.Copy).then_inc(fx_act, 1)

            def fox(step):
                h, s = divmod(step, 3)
                if s == 0:
                    act.wait_ge(fx_dve, 3 * h + 1)
                    op(fx_s[:, 0:P], fx_s[:, 0:P], ACT.Exp, bias=fx_m[:, 0:1], accum_out=fx_sum[:, 0:1])
                    op(fx_s[:, P:3 * P], fx_s[:, P:3 * P], ACT.Exp, bias=fx_m[:, 1:2], accum_out=fx_sum[:, 1:2]).then_inc(fx_act, 1)
                elif s == 1:
                    act.wait_ge(fx_pe, 4 + 3 * h + 2)
                    op(fx_pt[:, :], FB[:, 0:3 * P], ACT.Copy).then_inc(fx_act, 1)
                else:
                    act.wait_ge(fx_pe, 4 + 3 * h + 3)
                    op(oa_hi[:, h, :], FA[:, 0:T], ACT.Copy).then_inc(fx_act, 1)

            def gdn(step):
                half, unit, s = gdn_place(step)
                act.wait_ge(gd_pe, step + 1) if s in (0, 3, 5, 7, 9, 11, 13, 14) or (unit is None and chunk_of(s)[1]) else None
                d0 = gdn_base(half, unit, DVE_UNIT, DVE_HALF)
                if unit is None:
                    ch, second = chunk_of(s)
                    if second:
                        op(gdn_q[:, 4 * half:4 * half + 4, ch * CHUNK:(ch + 1) * CHUNK], GB[:, 0:4 * CHUNK], ACT.Copy).then_inc(gd_act, 1)
                    return
                h0 = 4 * half + 2 * unit
                if s == 0:
                    op(eg_b[:, :, :], GA[:, :], ACT.Exp).then_inc(gd_act, 1)
                    act.wait_ge(gd_dve, d0 + 1)
                    op(mt[:, :, :], mt[:, :, :], ACT.Exp).then_inc(gd_act, 1)
                elif s == 1:
                    act.wait_ge(gd_dve, d0 + 3)
                    op(lt[:, :, :], lt[:, :, :], ACT.Exp).then_inc(gd_act, 1)
                elif s in (3, 5, 7, 9, 11):
                    op(ys[:, :, :], GA[:, :], ACT.Copy).then_inc(gd_act, 1)
                elif s == 13:
                    for m in range(4):
                        h, p = h0 + m // 2, m % 2
                        op(ys[:, m, :], GB[:, m * P:(m + 1) * P], ACT.Copy, scale=beta_eg[:, p, h:h + 1])
                        i = op(gdn_k[:, h, p * P:(p + 1) * P], GB[:, m * P:(m + 1) * P], ACT.Copy, scale=k_dec[:, p, h:h + 1])
                    i.then_inc(gd_act, 1)
                elif s == 14:
                    op(gdn_v[:, h0:h0 + 2, :], GA[:, :], ACT.Copy)
                    op(w_t[:, 2 * unit:2 * unit + 2, :], GB[:, :], ACT.Copy).then_inc(gd_act, 1)

            def gdn_out(n):
                head_norm(n, NORM_OUT, gdn_q, 8)
                if n >= 2:
                    for pr in (2 * (n - 2), 2 * (n - 2) + 1):
                        act.wait_ge(nm_dve, NORM_OUT[2] + 2 + 2 * pr + 1)
                        op(ob_hi[:, 2 * pr:2 * pr + 2, :], gdn_q[:, 2 * pr:2 * pr + 2, :], ACT.Copy).then_inc(nm_act, 1)

            def mem_scale(t):
                act.wait_ge(mem_in[t], 16)
                op(junk[:, :], m_tok[:, :], ACT.Square, accum_out=ssum[:, 2 + t:3 + t]).then_inc(mm_act, 1)
                act.wait_ge(mm_dve, 10 * t + 1)
                rsqrt(rs_t[:, 2 + t:3 + t], ms_t[:, 2 + t:3 + t]).then_inc(mm_act, 1)

            def slots(s):
                if s == 0:
                    token_exps()
                if 0 <= s - GDN_N < 8:
                    if s == GDN_N:
                        act.wait_ge(silu_done, 6)
                    head_norm(s - GDN_N, NORM_GDN, gdn_all, 16)
                if 0 <= s - FOX_N < 8:
                    head_norm(s - FOX_N, NORM_FOX, fox_all, 16)
                if 0 <= s - CONF_S < 4:
                    conf_ln(s - CONF_S)
                if s == FOX_V:
                    fox_v_by_token()
                if fox_step(s) is not None:
                    fox(fox_step(s))
                if gdn_step(s) is not None:
                    gdn(gdn_step(s))
                if 0 <= s - GDN_OUT < 4:
                    if s == GDN_OUT:
                        act.wait_ge(y_added, 4)
                    gdn_out(s - GDN_OUT)
                for t in range(TT):
                    if s == MEM_LOAD[t]:
                        act.wait_ge(gd_pe, GDN_STEPS)
                        if t:
                            act.wait_ge(mm_pe, 4)
                        act.dma_start(m_tok[:, :], A["mem"][0, t * P:(t + 1) * P, :]).then_inc(mem_in[t], 16)
                    if s == MEM_S[t]:
                        mem_scale(t)
                    if 1 <= s - MEM_S[t] < 5:
                        k = s - MEM_S[t] - 1
                        act.wait_ge(mm_dve, 10 * t + 3 + 2 * k)
                        op(mem_hi[:, 4 * k:4 * k + 4, t * P:(t + 1) * P], split_t[:, :, :], ACT.Copy).then_inc(mm_act, 1)
                    if s == XR_LOAD[t]:
                        act.wait_ge(mm_pe, 8)
                        if t:
                            act.wait_ge(xr_pe, 4)
                        act.dma_start(xr_tok[:, :], A["x"][0, t * P:(t + 1) * P, :]).then_inc(xr_in[t], 16)
                    if 0 <= s - XR_S[t] < 4:
                        k = s - XR_S[t]
                        act.wait_ge(xr_pe, 4 * t + k + 1)
                        act.wait_ge(mm_dve, 20)
                        op(xres[:, 4 * k:4 * k + 4, t * P:(t + 1) * P], (FA, FB)[k % 2][:, :], ACT.Copy).then_inc(xr_act, 1)
                if 0 <= s - Y_SPLIT < 4:
                    g = s - Y_SPLIT
                    act.wait_ge(slab_used, Y_SPLIT)
                    act.wait_ge(y_added, 4 + g + 1)
                    op(act_hi[:, 4 * g:4 * g + 4, :], y[:, 4 * g:4 * g + 4, :], ACT.Copy, scale=0.5).then_inc(y_act, 1)

            def step(s, part):
                if s + LEAD < SLABS:
                    split(s + LEAD, (s + LEAD) % RING)
                part(s)

            def loop_split(n, j):
                split(n + (j + LEAD), (j + LEAD) % RING)

            for i in range(4):
                for j in range(8):
                    step(BASE["cu"] + 8 * i + j, slots)
                if i >= 2:
                    if i == 3:
                        act.wait_ge(group_read, 3)
                    act.wait_ge(slab_used, BASE["cu"] + 8 * i + 8)
                    op(gate[:, :, :], ps[i % 2][:, :, :], ACT.Tanh, scale=0.5).then_inc(tanh_out, 1)
            for i in range(6):
                n0 = BASE["gdn"] + 8 * i
                for j in range(8):
                    step(n0 + j, slots)
                act.wait_ge(slab_used, n0 + 8)
                for j in range(NT):
                    k = 4 * i + j
                    e = op(gdn_all[:, k, :], ps[i % 2][:, j, :], ACT.Copy, scale=col(C_GDN + (GDN_TAPS - 1) * 24 + k))
                e.then_inc(tanh_out, 1)
                act.wait_ge(group_read, READ["gdn"] + i + 1)
                op(gate[:, :, :], gdn_all[:, 4 * i:4 * i + 4, :], ACT.Tanh, scale=0.5).then_inc(tanh_out, 1)
            for i in range(6):
                for j in range(8):
                    step(BASE["fox"] + 8 * i + j, slots)

            def branch(name):
                for g in range(4):
                    n0 = BASE[name] + 12 * g
                    for j in range(8):
                        step(n0 + j, slots)
                    act.wait_ge(slab_used, n0 + 8)
                    if name == "brC":
                        act.wait_ge(cf_dve, 8)
                        act.wait_ge(group_read, READ[name] + g)
                    elif name == "brA" and g == 0:
                        act.wait_ge(group_read, READ[name])
                    else:
                        act.wait_ge(y_added, GATES[name] - 4 + g)
                    op(gate[:, :, :], ps[0][:, :, :], ACT.Tanh, scale=0.5).then_inc(gates_read, 1)
                    for j in range(8, 12):
                        step(n0 + j, slots)

            branch("brC")
            for i in range(2):
                for j in range(8):
                    step(BASE["z"] + 8 * i + j, slots)
                act.wait_ge(slab_used, BASE["z"] + 8 * i + 8)
                act.wait_ge(group_read, READ["z"] + i)
                op(gate[:, :, :], ps[i % 2][:, :, :], ACT.Tanh, scale=0.5).then_inc(tanh_out, 1)
            branch("brA")
            branch("brB")
            with act.Fori(0, 4) as g:
                for j in range(8):
                    loop_split(g * 8 + BASE["wout"], j)

            def x_norm(m, n):
                if n < 4:
                    if n:
                        act.wait_ge(mn_pe, 4 * m + n)
                    op(split_w[:, :, :], xres[:, 4 * n:4 * n + 4, :], ACT.Square).then_inc(mn_act, 1)
                elif n == 4:
                    act.wait_ge(mn_dve, 10 * m + 1)
                    rsqrt(rs_w[:, :], ms_w[:, :]).then_inc(mn_act, 1)
                else:
                    b = n - 5
                    act.wait_ge(mn_dve, 10 * m + 3 + 2 * b)
                    op(act_hi[:, 4 * b:4 * b + 4, :], split_w[:, :, :], ACT.Copy).then_inc(mn_act, 1)

            def late(s):
                if 0 <= s - NORM2 < 9:
                    if s == NORM2:
                        act.wait_ge(group_read, READ["wkv"])
                        act.wait_ge(slab_used, BASE["wkv"])
                    x_norm(0, s - NORM2)
                if s == XK_S:
                    act.wait_ge(mn_dve, 10)
                    act.wait_ge(group_read, READ["wkv"] + 1)
                    op(gate[:, :, :], xa_k[:, :, :], ACT.Square).then_inc(xa_act, 1)
                if s == XK_S + 1:
                    act.wait_ge(xa_dve, 1)
                    rsqrt(rs_w[0:16, :], ms_w[0:16, :]).then_inc(xa_act, 1)
                if s == XV_S:
                    act.wait_ge(xa_pe, 4)
                    for i in range(2):
                        e = op(xa_v[:, 2 * i:2 * i + 2, :], (GA, GB)[i][:, :], ACT.Copy)
                    e.then_inc(xa_act, 1)

            for s in range(BASE["wkv"], BASE["wo"]):
                step(s, late)
            act.wait_ge(group_read, READ["wq"] + 1)
            op(gate[:, :, :], xa_q[:, :, :], ACT.Square).then_inc(xa_act, 1)
            act.wait_ge(xa_dve, 5)
            rsqrt(rs_w[0:16, :], ms_w[0:16, :]).then_inc(xa_act, 1)
            for h in range(XA_H):
                act.wait_ge(xa_dve, 9 + h)
                for t in range(TT):
                    e = op(xa_p[:, h, t * T:(t + 1) * T], bk[h][:, t * T:(t + 1) * T], ACT.Exp, bias=xa_m[:, h, t:t + 1],
                           accum_out=xa_sum[:, h, t:t + 1])
                e.then_inc(xa_act, 1)
            for h in range(XA_H):
                act.wait_ge(xa_pe, 12 + h)
                op(xa_pt[:, h, :], bk[h][:, :], ACT.Copy).then_inc(xa_act, 1)
            for h in range(XA_H):
                act.wait_ge(xa_pe, 16 + h)
                op(xo_hi[:, h, :], bk[h][:, 0:T], ACT.Copy).then_inc(xa_act, 1)
            for s in range(BASE["wo"], BASE["up0"]):
                step(s, lambda s: None)
            act.wait_ge(group_read, READ["up0"])
            for n in range(9):
                x_norm(1, n)

            def conv_col(tap, half, g, j):
                a = C_FFW + tap * FT if tap is not None else C_FFB
                return par[:, bass.ds(g * NT + (a + 24 * half + j), 1)]

            done = 0
            for half, pairs in enumerate((6, 5)):
                r = READ[f"up{half}"]
                with act.Fori(0, pairs) as g:
                    n0 = g * 16 + BASE[f"up{half}"]
                    for j in range(8):
                        loop_split(n0, j)
                    act.wait_ge(slab_used, n0 + 8)
                    for j in range(NT):
                        e = op(ff_a[:, j, :], ps[0][:, j, :], ACT.Identity, scale=conv_col(2, half, g, j), bias=conv_col(None, half, g, j))
                    e.then_inc(ff_act, 1)
                    act.wait_ge(group_read, g * 2 + (r + 1))
                    op(ff_t[:, :, :], ff_a[:, :, :], ACT.Tanh, scale=0.5).then_inc(ff_act, 1)
                    for j in range(8):
                        loop_split(n0 + 8, j)
                    act.wait_ge(group_read, g * 2 + (r + 2))
                    op(g_hi[:, bass.ds(g * NT, NT), :], ff_a[:, :, :], ACT.Copy).then_inc(ff_act, 1)
                done += pairs
                per = 12 - 2 * half
                n0 = BASE[f"down{half}"]
                if not half:
                    with act.Fori(0, 4) as g:
                        for j in range(per):
                            loop_split(g * per + n0, j)
                else:
                    with act.Fori(0, 1) as g:
                        for j in range(2 * per):
                            loop_split(g * (2 * per) + n0, j)
                    for j in range(2 * per - LEAD):
                        loop_split(n0 + 2 * per, j)
            for b in range(8):
                g, t = divmod(b, 2)
                act.wait_ge(fin_pe, b + 1)
                op(out_tok[:, t, 4 * g * P:4 * (g + 1) * P], bk[b % 4][:, :], ACT.Copy).then_inc(fin_act, 1)

        @block.vector
        def _(dve):
            own = Order(dve, dve_own)
            v = nc.vector
            stt, tsc, tt_ = v.scalar_tensor_tensor, v.tensor_scalar, v.tensor_tensor

            def split(n, slot):
                dve.wait_ge(slab_hi, n + 1)
                tt_(w_lo[:, slot, :, :], w_f[:, slot, :, :], w_hi[:, slot, :, :].bitcast(F32), ALU.subtract).then_inc(slab_lo, 1)

            def newton(r, ms, tmp):
                own.then(tt_(tmp, r, r, ALU.mult))
                own.then(stt(tmp, tmp, -0.5, ms, ALU.mult, ALU.mult))
                return stt(r, tmp, 1.5, r, ALU.add, ALU.mult)

            dve.wait_ge(pre_pe, 6)
            for b, n in enumerate(PB):
                e = v.tensor_copy(par[:, PO[b]:PO[b] + n], bk[b // 3][:, (b % 3) * P:(b % 3) * P + n])
            e.then_inc(pre_dve, 1)
            for t in range(TT):
                cl = slice(t, t + 1)
                dve.wait_ge(pre_act, 2 * t + 1)
                tsc(ms_t[:, cl], ssum[:, cl], 1.0 / D, EPS, ALU.mult, ALU.add).then_inc(pre_dve, 1)
                dve.wait_ge(pre_act, 2 * t + 2)
                own.then(newton(rs_t[:, cl], ms_t[:, cl], tmp_t[:, cl]))
                tsc(x_tok[:, t, :], x_tok[:, t, :], rs_t[:, cl], None, ALU.mult).then_inc(pre_dve, 1)
            for b in range(8):
                t, k = divmod(b, 4)
                dve.wait_ge(pre_pe, 7 + b)
                gains = par[:, G_MIX + 4 * k:G_MIX + 4 * k + 4].unsqueeze(2).to_broadcast([P, 4, P])
                tt_(split_t[:, :, :], bk[2 + b % 2][:, :].rearrange("p (a b) -> p a b", a=4), gains, ALU.mult).then_inc(pre_dve, 1)
                dve.wait_ge(pre_dve, 6 + b)
                dve.wait_ge(pre_act, 5 + b)
                cols = (slice(None), slice(4 * k, 4 * k + 4), slice(t * P, (t + 1) * P))
                tt_(act_lo[cols], split_t[:, :, :], act_hi[cols].bitcast(F32), ALU.subtract).then_inc(h_ready, 1)
                if b == 3:
                    for n in range(LEAD):
                        split(n, n)
                dve.wait_ge(h_ready, b + 1)
            dve.wait_ge(pre_act, 13)
            tt_(nar_lo[:, :, :], nar_f[:, :, :], nar_hi[:, :, :].bitcast(F32), ALU.subtract).then_inc(pre_dve, 1)
            dve.wait_ge(pre_pe, 15)
            own.then(v.tensor_copy(nar[:, :, :], FA[:, 0:48].rearrange("p (a b) -> p a b", a=TT)))
            dve.wait_ge(bias_in, 48)
            stt(sp_v[:, :, 0:8], nar[:, :, 0:8], -1.0, over(bias24[:, 0:8], TT), ALU.mult, ALU.subtract)
            tt_(sp_v[:, :, 8:16], nar[:, :, 8:16], over(bias24[:, 8:16], TT), ALU.add)
            tsc(sp_v[:, :, 16:24], nar[:, :, 16:24], -1.0, None, ALU.mult).then_inc(pre_dve, 1)
            dve.wait_ge(pre_dve, 15)
            dve.wait_ge(pre_act, 14)
            own.then(stt(sp_v[:, :, :], sp_v[:, :, :], 0.0, sp_a[:, :, :], ALU.max, ALU.add))
            v.tensor_copy(logf_n[:, :, :], sp_v[:, :, 0:8])
            stt(gdn_g[:, :, :], sp_v[:, :, 8:16], -1.0, over(bias24[:, 16:24], TT), ALU.mult, ALU.mult)
            tsc(ln_beta[:, :, :], sp_v[:, :, 16:24], -1.0, None, ALU.mult).then_inc(pre_dve, 1)

            def token_columns():
                dve.wait_ge(pre_dve, 16)
                dve.wait_ge(pre_pe, 16)

                def by(a):
                    return FB[:, a:a + 16].rearrange("p (a b) -> p a b", a=TT)
                tsc(f_col[:, :, :], by(0), -1.0, None, ALU.mult)
                tsc(g_neg[:, :, :], by(16), -1.0, None, ALU.mult)
                tt_(beta_eg[:, :, :], by(16), ln_beta[:, :, :], ALU.add).then_inc(pre_dve, 1)
                dve.wait_ge(pre_act, 15)
                tsc(half_beta[:, :, :], half_beta[:, :, :], 0.5, None, ALU.mult)
                tsc(qgain[:, 0:1], col(G_FQ), HD ** -0.5, None, ALU.mult)
                tsc(qgain[:, 1:2], col(G_XQ), HD ** -0.5, None, ALU.mult).then_inc(pre_dve, 1)
                dve.wait_ge(pre_dve, 18)

            def head_norm(n, events, region, tiles, acc, banks, scale, gain, after=None):
                p0, a0, d0 = events
                nb = tiles // 4
                if n == nb - 1:
                    dve.wait_ge(nm_pe, p0 + nb)
                    tsc(ms_w[0:16, :], acc[0:16, 0:T], scale, EPS, ALU.mult, ALU.add).then_inc(nm_dve, 1)
                if n < nb:
                    return
                if n == nb:
                    dve.wait_ge(nm_act, a0 + nb + 1)
                    newton(rs_w[0:16, :], ms_w[0:16, :], tmp_w[0:16, :]).then_inc(nm_dve, 1)
                for pr in (2 * (n - nb), 2 * (n - nb) + 1):
                    dve.wait_ge(nm_pe, p0 + nb + pr + 1)
                    two = region[:, 2 * pr:2 * pr + 2, :]
                    e = stt(two, two, gain(2 * pr), banks[pr % 2][:, :].rearrange("p (a b) -> p a b", a=2), ALU.mult, ALU.mult)
                    if after is None:
                        e.then_inc(nm_dve, 1)
                    else:
                        after(pr, own.then(e))

            def conf_taps(s):
                total = CT * CONF_TAPS
                n = s - CONV_S
                for i in range(total * n // CONV_SLOTS, total * (n + 1) // CONV_SLOTS):
                    k, back = divmod(i, CONF_TAPS)
                    w = col(C_CONF + (CONF_TAPS - 1 - back) * CT + k)
                    if back == 0:
                        own.then(tsc(conf[:, k, :], cu_a[:, k, :], w, None, ALU.mult))
                    else:
                        e = stt(conf[:, k, back:T], cu_a[:, k, 0:T - back], w, conf[:, k, back:T], ALU.mult, ALU.add)
                        if i == total - 1:
                            e.then_inc(cf_dve, 1)
                        else:
                            own.then(e)

            def conf_ln(n):
                if n == 0:
                    dve.wait_ge(cf_pe, 1)
                    mean = FA[:, 0:T].unsqueeze(1).to_broadcast([P, 4, T])
                    for k in range(2):
                        e = stt(conf[:, 4 * k:4 * k + 4, :], mean, -1.0 / CONV_CH, conf[:, 4 * k:4 * k + 4, :], ALU.mult, ALU.add)
                    e.then_inc(cf_dve, 1)
                elif n == 2:
                    dve.wait_ge(cf_pe, 3)
                    tsc(ms_w[:, :], FA[:, T:2 * T], 1.0 / CONV_CH, LN_EPS, ALU.mult, ALU.add).then_inc(cf_dve, 1)
                elif n == 3:
                    dve.wait_ge(cf_act, 4)
                    own.then(newton(rs_w[:, :], ms_w[:, :], tmp_w[:, :]))
                    rs = over(rs_w[:, :], 4)
                    for k in range(2):
                        e = tt_(conf[:, 4 * k:4 * k + 4, :], conf[:, 4 * k:4 * k + 4, :], rs, ALU.mult)
                    e.then_inc(cf_dve, 1)
                    for hf in range(2):
                        half = (slice(None), slice(4 * hf, 4 * hf + 4), slice(None))
                        dve.wait_ge(cf_act, 6 + 2 * hf)
                        stt(conf[half], gate[:, :, :], 1.0, conf[half], ALU.add, ALU.mult).then_inc(cf_dve, 1)
                        dve.wait_ge(cf_act, 7 + 2 * hf)
                        stt(oc_lo[half], conf[half], 0.5, oc_hi[half].bitcast(F32), ALU.mult, ALU.subtract).then_inc(cf_dve, 1)

            def fox(step):
                h, s = divmod(step, 3)
                if s == 0:
                    dve.wait_ge(fx_pe, 4 + 3 * h + 1)
                    stt(fx_s[:, 0:P], FA[:, 0:P], f_col[:, 0, h:h + 1], c("not_causal"), ALU.add, ALU.add)
                    own.then(stt(fx_s[:, P:3 * P], FA[:, P:3 * P], f_col[:, 1, h:h + 1], zero_causal, ALU.add, ALU.add))
                    v.reduce_max(fx_m[:, 0:1], fx_s[:, 0:P], AX.X)
                    own.then(v.reduce_max(fx_m[:, 1:2], fx_s[:, P:3 * P], AX.X))
                    tsc(fx_m[:, :], fx_m[:, :], -1.0, None, ALU.mult).then_inc(fx_dve, 1)
                    dve.wait_ge(fx_act, 4 + 3 * h + 1)
                    own.then(v.reciprocal(fx_sum[:, :], fx_sum[:, :]))
                    tsc(fx_s[:, 0:P], fx_s[:, 0:P], fx_sum[:, 0:1], None, ALU.mult)
                    tsc(fx_s[:, P:3 * P], fx_s[:, P:3 * P], fx_sum[:, 1:2], None, ALU.mult).then_inc(fx_dve, 1)
                elif s == 2:
                    dve.wait_ge(fx_act, 4 + 3 * h + 3)
                    tt_(oa_lo[:, h, :], FA[:, 0:T], oa_hi[:, h, :].bitcast(F32), ALU.subtract).then_inc(fx_dve, 1)

            def gdn(step):
                half, unit, s = gdn_place(step)
                a0 = gdn_base(half, unit, ACT_UNIT, ACT_HALF)
                if unit is None:
                    gdn_chain(half, step, s)
                    return
                h0 = 4 * half + 2 * unit
                mats = [(2 * i + p, h0 + i, p) for i in range(2) for p in range(2)]

                def o(bank, m):
                    return bank[:, m * P:(m + 1) * P]

                def by4(bank):
                    return bank[:, :].rearrange("p (a b) -> p a b", a=4)

                def level(lv):
                    return tt_(mt[:, :, :], lt[:, :, :], over(c(f"level{lv}"), 4), ALU.mult)

                if s in (0, 1, 2, 4, 6, 8, 10, 12, 13):
                    dve.wait_ge(gd_pe, step + 1)
                if step == 0:
                    dve.wait_ge(nm_dve, NORM_FOX[2])
                if s == 0:
                    dve.wait_ge(gd_act, a0 + 1)
                    for m, h, p in mats:
                        e = stt(mt[:, m, :], o(GA, m), g_neg[:, p, h:h + 1], c("not_before"), ALU.add, ALU.add)
                    e.then_inc(gd_dve, 1)
                    dve.wait_ge(gd_act, a0 + 2)
                    tt_(attn_t[:, 2 * unit:2 * unit + 2, :], GB[:, :].rearrange("p (a b) -> p a b", a=2),
                        mt[:, :, :].rearrange("p (a c) b -> p a (c b)", a=2), ALU.mult)
                    eg = eg_b[:, :, :].rearrange("p (a c) b -> p a (c b)", a=2)
                    v.tensor_copy(g_last[:, h0:h0 + 2, :], eg[:, :, CHUNK - 1::CHUNK])
                    tt_(gdn_q[:, h0:h0 + 2, :], gdn_q[:, h0:h0 + 2, :], eg, ALU.mult).then_inc(gd_dve, 1)
                elif s == 1:
                    for m, h, p in mats:
                        e = stt(lt[:, m, :], o(GA, m), g_neg[:, p, h:h + 1], c("not_strict"), ALU.add, ALU.add)
                    e.then_inc(gd_dve, 1)
                    dve.wait_ge(gd_act, a0 + 3)
                    own.then(tt_(lt[:, :, :], by4(GB), lt[:, :, :], ALU.mult))
                    own.then(level(0))
                    tt_(tinv_t[:, :, :], over(ident, 4), mt[:, :, :], ALU.subtract).then_inc(gd_dve, 1)
                elif s == 2:
                    tt_(tinv[:, :, :], over(ident, 4), by4(GA), ALU.subtract)
                    level(1).then_inc(gd_dve, 1)
                elif s in (4, 6, 8, 10, 12):
                    lv = (s - 2) // 2
                    if lv < 5:
                        tt_(tinv[:, :, :], tinv[:, :, :], by4(GB), ALU.subtract)
                        tt_(tinv_t[:, :, :], tinv_t[:, :, :], by4(GA), ALU.subtract)
                        level(lv + 1).then_inc(gd_dve, 1)
                    else:
                        tt_(tinv_t[:, :, :], tinv_t[:, :, :], by4(GA), ALU.subtract).then_inc(gd_dve, 1)
                elif s == 13:
                    for m, h, p in mats:
                        e = tsc(mt[:, m, :], o(GA, m), half_beta[:, p, h:h + 1], None, ALU.mult)
                    e.then_inc(gd_dve, 1)

            def gdn_chain(half, step, s):
                ch, second = chunk_of(s)
                p, r = ch // 2, slice((ch % 2) * CHUNK, (ch % 2 + 1) * CHUNK)
                dve.wait_ge(gd_pe, step + 1)
                if not second:
                    tt_(vnew[r, :, :], gdn_v[r, 4 * half:4 * half + 4, p * P:(p + 1) * P],
                        GA[r, :].rearrange("p (a b) -> p a b", a=4), ALU.subtract).then_inc(gd_dve, 1)
                elif ch == 0:
                    v.tensor_copy(state[:, :, :], GA[:, :].rearrange("p (a b) -> p a b", a=4)).then_inc(gd_dve, 1)
                elif ch < NCHUNK - 1:
                    for i4 in range(4):
                        e = stt(state[:, i4, :], state[:, i4, :], g_last[:, 4 * half + i4, ch:ch + 1], GA[:, i4 * P:(i4 + 1) * P], ALU.mult, ALU.add)
                    e.then_inc(gd_dve, 1)

            def gdn_gate(pr, _):
                two = (slice(None), slice(2 * pr, 2 * pr + 2), slice(None))
                stt(gdn_q[two], gdn_q[two], 0.5, z_act[two], ALU.mult, ALU.mult).then_inc(nm_dve, 1)
                dve.wait_ge(nm_act, NORM_OUT[1] + 3 + pr + 1)
                tt_(ob_lo[two], gdn_q[two], ob_hi[two].bitcast(F32), ALU.subtract).then_inc(nm_dve, 1)

            def mem_scale(t):
                cl = slice(2 + t, 3 + t)
                dve.wait_ge(mm_act, 6 * t + 1)
                tsc(ms_t[:, cl], ssum[:, cl], 1.0 / D, EPS, ALU.mult, ALU.add).then_inc(mm_dve, 1)
                dve.wait_ge(mm_act, 6 * t + 2)
                own.then(newton(rs_t[:, cl], ms_t[:, cl], tmp_t[:, cl]))
                tsc(m_tok[:, :], m_tok[:, :], rs_t[:, cl], None, ALU.mult).then_inc(mm_dve, 1)

            def mem_batch(t, k):
                dve.wait_ge(mm_pe, 4 * t + k + 1)
                gains = par[:, G_MEM + 4 * k:G_MEM + 4 * k + 4].unsqueeze(2).to_broadcast([P, 4, P])
                tt_(split_t[:, :, :], FA[:, :].rearrange("p (a b) -> p a b", a=4), gains, ALU.mult).then_inc(mm_dve, 1)
                dve.wait_ge(mm_act, 6 * t + 3 + k)
                cols = (slice(None), slice(4 * k, 4 * k + 4), slice(t * P, (t + 1) * P))
                tt_(mem_lo[cols], split_t[:, :, :], mem_hi[cols].bitcast(F32), ALU.subtract).then_inc(mm_dve, 1)

            def slots(s):
                if s == 0:
                    token_columns()
                if 0 <= s - CONV_S < CONV_SLOTS:
                    conf_taps(s)
                if 0 <= s - GDN_N < 8:
                    head_norm(s - GDN_N, NORM_GDN, gdn_all, 16, GA, (GA, GB), 0.25, lambda i: 0.5 * HD ** -0.5 if i < 8 else 0.5)
                if 0 <= s - FOX_N < 8:
                    head_norm(s - FOX_N, NORM_FOX, fox_all, 16, FA, (FA, FB), 1.0 / HD, lambda i: qgain[:, 0:1] if i < 8 else col(G_FK))
                if 0 <= s - CONF_S < 4:
                    conf_ln(s - CONF_S)
                if fox_step(s) is not None:
                    fox(fox_step(s))
                if gdn_step(s) is not None:
                    gdn(gdn_step(s))
                if 0 <= s - GDN_OUT < 4:
                    head_norm(s - GDN_OUT, NORM_OUT, gdn_q, 8, GA, (GA, GB), 1.0 / HD, lambda i: col(G_GO), after=gdn_gate)
                for t in range(TT):
                    if s == MEM_S[t]:
                        mem_scale(t)
                    if 1 <= s - MEM_S[t] < 5:
                        mem_batch(t, s - MEM_S[t] - 1)
                if 0 <= s - Y_SPLIT < 4:
                    g = s - Y_SPLIT
                    if g == 3:
                        return
                    y_split(g)

            def y_split(g):
                dve.wait_ge(y_act, g + 1)
                four = (slice(None), slice(4 * g, 4 * g + 4), slice(None))
                stt(act_lo[four], y[four], 0.5, act_hi[four].bitcast(F32), ALU.mult, ALU.subtract).then_inc(y_ready, 1)

            def step(s, part):
                if s + LEAD < SLABS:
                    split(s + LEAD, (s + LEAD) % RING)
                part(s)

            def loop_split(n, j):
                split(n + (j + LEAD), (j + LEAD) % RING)

            for i in range(4):
                n0 = BASE["cu"] + 8 * i
                for j in range(8):
                    step(n0 + j, slots)
                dve.wait_ge(slab_used, n0 + 8)
                if i < 2:
                    v.tensor_copy(cu_a[:, 4 * i:4 * i + 4, :], ps[i % 2][:, :, :]).then_inc(group_read, 1)
                else:
                    dve.wait_ge(tanh_out, i - 1)
                    a = cu_a[:, 4 * i - 8:4 * i - 4, :]
                    stt(a, gate[:, :, :], 1.0, a, ALU.add, ALU.mult).then_inc(group_read, 1)
            dve.wait_ge(group_read, 4)
            for i in range(6):
                n0 = BASE["gdn"] + 8 * i
                for j in range(8):
                    step(n0 + j, slots)
                dve.wait_ge(tanh_out, 2 + 2 * i + 1)
                for back in range(1, GDN_TAPS):
                    for j in range(NT):
                        k = 4 * i + j
                        w = col(C_GDN + (GDN_TAPS - 1 - back) * 24 + k)
                        o = gdn_all[:, k, back:T]
                        e = stt(o, ps[i % 2][:, j, 0:T - back], w, o, ALU.mult, ALU.add)
                        if j == NT - 1 and back < GDN_TAPS - 1:
                            own.then(e)
                e.then_inc(group_read, 1)
                dve.wait_ge(tanh_out, 2 + 2 * i + 2)
                four = gdn_all[:, 4 * i:4 * i + 4, :]
                stt(four, gate[:, :, :], 1.0, four, ALU.add, ALU.mult).then_inc(silu_done, 1)
                dve.wait_ge(silu_done, i + 1)
            for i in range(6):
                n0 = BASE["fox"] + 8 * i
                for j in range(8):
                    step(n0 + j, slots)
                dve.wait_ge(slab_used, n0 + 8)
                v.tensor_copy(fox_all[:, 4 * i:4 * i + 4, :], ps[i % 2][:, :, :]).then_inc(group_read, 1)

            def branch(name):
                for g in range(4):
                    n0 = BASE[name] + 12 * g
                    for j in range(12):
                        step(n0 + j, slots)
                    dve.wait_ge(slab_used, n0 + 12)
                    dve.wait_ge(gates_read, GATES[name] + g + 1)
                    four = y[:, 4 * g:4 * g + 4, :]
                    o = four if name == "brC" else gate[:, :, :]
                    stt(o, gate[:, :, :], 1.0, ps[1][:, :, :], ALU.add, ALU.mult).then_inc(group_read, 1)
                    if name != "brC":
                        dve.wait_ge(group_read, READ[name] + g + 1)
                        tt_(four, four, gate[:, :, :], ALU.add).then_inc(y_added, 1)

            branch("brC")
            for i in range(2):
                n0 = BASE["z"] + 8 * i
                for j in range(8):
                    step(n0 + j, slots)
                if i == 0:
                    dve.wait_ge(fx_pe, 4 + FOX_STEPS)
                dve.wait_ge(tanh_out, 14 + i + 1)
                stt(z_act[:, 4 * i:4 * i + 4, :], gate[:, :, :], 1.0, ps[i % 2][:, :, :], ALU.add, ALU.mult).then_inc(group_read, 1)
            branch("brA")
            branch("brB")
            y_split(3)
            dve.wait_ge(xr_act, 8)
            with dve.Fori(0, 2) as g:
                for k in range(2):
                    n0 = g * 16 + (BASE["wout"] + 8 * k)
                    for j in range(8):
                        loop_split(n0, j)
                    dve.wait_ge(slab_used, n0 + 8)
                    four = xres[:, bass.ds(g * 8 + 4 * k, 4), :]
                    tt_(four, four, ps[k][:, :, :], ALU.add).then_inc(group_read, 1)

            def x_norm(m, n, gain):
                if n == 3:
                    dve.wait_ge(mn_pe, 4 * m + 4)
                    tsc(ms_w[:, :], FA[:, 0:T], 1.0 / D, EPS, ALU.mult, ALU.add).then_inc(mn_dve, 1)
                elif n == 4:
                    dve.wait_ge(mn_act, 9 * m + 5)
                    newton(rs_w[:, :], ms_w[:, :], tmp_w[:, :]).then_inc(mn_dve, 1)
                    dve.wait_ge(mn_dve, 10 * m + 2)
                elif n > 4:
                    b = n - 5
                    for j in range(4):
                        e = stt(split_w[:, j, :], xres[:, 4 * b + j, :], col(gain + 4 * b + j), rs_w[:, :], ALU.mult, ALU.mult)
                    e.then_inc(mn_dve, 1)
                    dve.wait_ge(mn_act, 9 * m + 6 + b)
                    four = (slice(None), slice(4 * b, 4 * b + 4), slice(None))
                    tt_(act_lo[four], split_w[:, :, :], act_hi[four].bitcast(F32), ALU.subtract).then_inc(mn_dve, 1)
                    dve.wait_ge(mn_dve, 10 * m + 4 + 2 * b)

            def xa_norm(d, region, gain, stage):
                if stage == 0:
                    tsc(ms_w[0:16, :], FA[0:16, 0:T], 1.0 / HD, EPS, ALU.mult, ALU.add).then_inc(xa_dve, 1)
                else:
                    newton(rs_w[0:16, :], ms_w[0:16, :], tmp_w[0:16, :]).then_inc(xa_dve, 1)
                    for pr in range(2):
                        dve.wait_ge(xa_pe, (2 if d == 0 else 6) + pr)
                        two = region[:, 2 * pr:2 * pr + 2, :]
                        stt(two, two, gain, (FA, FB)[pr][:, :].rearrange("p (a b) -> p a b", a=2), ALU.mult, ALU.mult).then_inc(xa_dve, 1)

            def late(s):
                if 0 <= s - NORM2 < 9:
                    x_norm(0, s - NORM2, G_XA)
                if s == XK_S:
                    dve.wait_ge(xa_pe, 1)
                    xa_norm(0, xa_k, None, 0)
                if s == XK_S + 1:
                    dve.wait_ge(xa_act, 2)
                    xa_norm(0, xa_k, col(G_XK), 1)

            for i, (name, dst) in enumerate((("wkv", xa_k), ("wkv", xa_v), ("wq", xa_q))):
                n0 = BASE["wkv"] + 8 * i
                for j in range(8):
                    step(n0 + j, late)
                dve.wait_ge(slab_used, n0 + 8)
                v.tensor_copy(dst[:, :, :], ps[i % 2][:, :, :]).then_inc(group_read, 1)
            dve.wait_ge(xa_pe, 5)
            xa_norm(4, xa_q, None, 0)
            dve.wait_ge(xa_act, 5)
            xa_norm(4, xa_q, qgain[:, 1:2], 1)
            for h in range(XA_H):
                dve.wait_ge(xa_pe, 8 + h)
                own.then(v.reduce_max(xa_m[:, h, :], bk[h][:, :].rearrange("p (a b) -> p a b", a=TT), AX.X))
                tsc(xa_m[:, h, :], xa_m[:, h, :], -1.0, None, ALU.mult).then_inc(xa_dve, 1)
            for h in range(XA_H):
                dve.wait_ge(xa_act, 6 + h)
                own.then(v.reciprocal(xa_sum[:, h, :], xa_sum[:, h, :]))
                for t in range(TT):
                    pt = xa_p[:, h, t * T:(t + 1) * T]
                    e = tsc(pt, pt, xa_sum[:, h, t:t + 1], None, ALU.mult)
                e.then_inc(xa_dve, 1)
            for h in range(XA_H):
                dve.wait_ge(xa_act, 14 + h)
                tt_(xo_lo[:, h, :], bk[h][:, 0:T], xo_hi[:, h, :].bitcast(F32), ALU.subtract).then_inc(xa_dve, 1)
            for i in range(4):
                n0 = BASE["wo"] + 2 * i
                for j in range(2):
                    step(n0 + j, lambda s: None)
                dve.wait_ge(slab_used, n0 + 2)
                four = xres[:, 4 * i:4 * i + 4, :]
                tt_(four, four, ps[i % 2][:, :, :], ALU.add).then_inc(group_read, 1)
            dve.wait_ge(group_read, READ["up0"])
            for n in range(9):
                x_norm(1, n, G_FFN)

            def conv_col(tap, half, g, j):
                return par[:, bass.ds(g * NT + (C_FFW + tap * FT + 24 * half + j), 1)]

            done = 0
            for half, pairs in enumerate((6, 5)):
                with dve.Fori(0, pairs) as g:
                    own.enter(g, 2)
                    n0 = g * 16 + BASE[f"up{half}"]
                    for j in range(8):
                        loop_split(n0, j)
                    dve.wait_ge(ff_act, g * 3 + (3 * done + 1))
                    for back in range(1, FFN_TAPS):
                        for j in range(NT):
                            o = ff_a[:, j, back:T]
                            e = stt(o, ps[0][:, j, 0:T - back], conv_col(FFN_TAPS - 1 - back, half, g, j), o, ALU.mult, ALU.add)
                        if back == 1:
                            own.then(e)
                    e.then_inc(group_read, 1)
                    dve.wait_ge(ff_act, g * 3 + (3 * done + 2))
                    own.then(stt(ff_a[:, :, :], ff_t[:, :, :], 1.0, ff_a[:, :, :], ALU.add, ALU.mult))
                    for j in range(8):
                        loop_split(n0 + 8, j)
                    dve.wait_ge(slab_used, n0 + 16)
                    stt(ff_a[:, :, :], ff_a[:, :, :], 0.5, ps[1][:, :, :], ALU.mult, ALU.mult).then_inc(group_read, 1)
                    dve.wait_ge(ff_act, g * 3 + (3 * done + 3))
                    tt_(g_lo[:, bass.ds(g * NT, NT), :], ff_a[:, :, :], g_hi[:, bass.ds(g * NT, NT), :].bitcast(F32), ALU.subtract)\
                        .then_inc(g_ready, 1)
                    own.leave_body()
                own.leave(pairs)
                done += pairs
                per = 12 - 2 * half
                n0 = BASE[f"down{half}"]

                def add(n_end, k, at):
                    dve.wait_ge(slab_used, n_end)
                    four = xres[:, at, :]
                    tt_(four, four, ps[k][:, :, :], ALU.add).then_inc(group_read, 1)

                with dve.Fori(0, 2 - half) as g:
                    for k in range(2):
                        for j in range(per):
                            loop_split(g * (2 * per) + n0, k * per + j)
                        add(g * (2 * per) + (n0 + (k + 1) * per), k, bass.ds(g * 8 + 4 * k, 4))
                if half:
                    for k in range(2):
                        for j in range(per):
                            if 2 * per + k * per + j + LEAD < 4 * per:
                                loop_split(n0 + 2 * per, k * per + j)
                        add(n0 + (3 + k) * per, k, slice(8 + 4 * k, 12 + 4 * k))


_INS = ["x", "mem", "mix_norm_g", "w_in", "fox_fb", "fox_q_norm_g", "fox_k_norm_g", "gdn_conv_w", "gdn_a_log",
        "gdn_dt_bias", "gdn_out_norm_g", "conf_dw_w", "conf_dw_b", "conf_ln_g", "conf_ln_b", "w_branch", "w_out",
        "mem_norm_g", "xattn_norm_g", "xattn_wq", "xattn_wkv", "xattn_q_norm_g", "xattn_k_norm_g", "xattn_wo",
        "ffn_norm_g", "ffn_w_up", "ffn_conv_w", "ffn_conv_b", "ffn_w_down"]


def kernel(**inputs):
    import concourse.bacc as bacc
    from concourse.bass_utils import run_bass_kernel_spmd

    nc = bacc.Bacc("TRN2", target_bir_lowering=False, num_devices=1)
    arrays, aps = {}, {}
    for name in _INS + ["const"]:
        a = np.ascontiguousarray(CONST if name == "const" else inputs[name])
        arrays[f"in_{name}"] = a
        aps[name] = nc.dram_tensor(f"in_{name}", a.shape, mybir.dt.from_np(a.dtype), kind="ExternalInput").ap()
    out = nc.dram_tensor("out_x", (1, T, D), F32, kind="ExternalOutput").ap()
    build(nc, aps, out)
    r = run_bass_kernel_spmd(nc, [arrays], core_ids=[0])
    return r.results[0]["out_x"]
```

```python
import numpy as np
import concourse.bass as bass
from concourse import mybir
from contextlib import ExitStack

F32 = mybir.dt.float32
F32R = mybir.dt.float32r
ACT = mybir.ActivationFunctionType
ALU = mybir.AluOpType
AX = mybir.AxisListType

P = 128
T = 256
TT = T // P
D = 2048
DT = D // P
HD = 128
FOX_H = 8
GDN_H = 8
CONV_CH = 1024
CT = CONV_CH // P
BR_T = 1024 // P
GDN_TAPS = 4
CONF_TAPS = 31
FFN_TAPS = 3
D_FF = 5632
FT = D_FF // P
XA_H = 4
CHUNK = 64
NCHUNK = T // CHUNK
EPS = 1e-6
LN_EPS = 1e-5
BIG = -1.0e30

FOX_C = 0
FF_C = 3 * FOX_H * HD
GDN_C = FF_C + FOX_H
GAB_C = GDN_C + 3 * GDN_H * HD
Z_C = GAB_C + 2 * GDN_H
CU_C = Z_C + GDN_H * HD
GL_C = CU_C + 2 * CONV_CH

KS = 2
NC = 512
NT = NC // P
RING = 4
LEAD = 3

PHASES = [("cu", 4, 8), ("gdn", 6, 8), ("fox", 6, 8), ("brC", 4, 12), ("z", 2, 8), ("brA", 4, 12),
          ("brB", 4, 12), ("wout", 4, 8), ("wkv", 2, 8), ("wq", 1, 8), ("wo", 4, 2),
          ("up0", 12, 8), ("down0", 4, 12), ("up1", 10, 8), ("down1", 4, 10)]
BASE = {}
_n = 0
for _name, _g, _s in PHASES:
    BASE[_name] = _n
    _n += _g * _s
SLABS = _n

READ = {}
_n = 0
for _name, _g, _s in PHASES:
    READ[_name] = _n
    _n += _g
GATES = {"brC": 0, "brA": 4, "brB": 8}

def constants():
    t = np.arange(P)
    a, b = t[:, None], t[None, :]
    same = (a // CHUNK) == (b // CHUNK)
    parts = [
        ("ident", (a == b)),
        ("upto", (a <= b)),
        ("ones", np.ones((P, P))),
        ("chunk_upto", (a <= b) & same),
        ("chunk_after", (a > b) & same),
        ("not_before", np.where((a <= b) & same, 0.0, BIG)),
        ("not_strict", np.where((a < b) & same, 0.0, BIG)),
        ("zero", np.zeros((P, P))),
        ("not_causal", np.where(b <= a, 0.0, BIG)),
    ]
    for lv in range(6):
        w = 1 << lv
        m = ((a // (2 * w)) == (b // (2 * w))) & ((b // w) % 2 == 1) & ((a // w) % 2 == 0)
        parts.append((f"level{lv}", m))
    pick = np.zeros((P, 32))
    pick[:, 15] = 1.0
    parts.append(("pick", pick))
    at, off = {}, 0
    for name, m in parts:
        at[name] = (off, off + m.shape[1])
        off += m.shape[1]
    return np.concatenate([m.astype(np.float32) for _, m in parts], axis=1), at


CONST, CONST_AT = constants()

PB = [93, 96, 128, 120, 88, 88]
PO = [sum(PB[:i]) for i in range(len(PB) + 1)]
G_MIX, G_MEM, G_XA, G_FFN = 0, 16, 32, 48
C_DWB, C_LNG, C_LNB = 64, 72, 80
G_FQ, G_FK, G_GO, G_XQ, G_XK = 88, 89, 90, 91, 92
C_GDN = PO[1]
C_CONF = PO[2]
C_FFW = PO[4]
C_FFB = C_FFW + FFN_TAPS * FT

X_S = (1, 3)
NARROW_S = 8
TOKEN_S = 11
SILU_J = 4
CONV_SLOTS = [s for s in range(BASE["gdn"], BASE["brC"] - 1)
              if s < BASE["gdn"] + 8 or s >= BASE["fox"] + 8 or s % 8 not in (0, 1, 2, 4)]
CONF_S = BASE["brC"]
GDN_N = BASE["fox"] + 5
GDN_S = GDN_N + 9
FOX_N = BASE["fox"] + 34
FOX_V = BASE["brC"] + 7
FOX_S = FOX_V + 2
UNIT_STEPS = 15
HALF_STEPS = 2 * UNIT_STEPS + 7
GDN_STEPS = 2 * HALF_STEPS
FOX_STEPS = 3 * FOX_H
GDN_OUT = BASE["brB"]
MEM_LOAD = [BASE["brB"] + 5, BASE["brB"] + 17]
MEM_S = [BASE["brB"] + 8, BASE["brB"] + 20]
MEM_BATCH = (2, 4, 6, 8)
XR_LOAD = [BASE["brB"] + 29, BASE["brB"] + 36]
XR_S = [BASE["brB"] + 32, BASE["brB"] + 39]
Y_SPLIT = BASE["brB"] + 44
NORM2 = BASE["wkv"]
XK_S = BASE["wkv"] + 11
XV_S = BASE["wq"]
OUT_S = [BASE["down1"] + 21, BASE["down1"] + 25, BASE["down1"] + 33]

X_SCALED, X_LOW = (3, 4, 6, 8), (5, 7, 9, 10)

NORM_GDN, NORM_FOX, NORM_OUT = (0, 0, 0), (12, 5, 10), (24, 10, 20)
NORM_END = (30, 17, 30)


def gdn_step(slot):
    n = slot - GDN_S
    return n // 2 if n >= 0 and n % 2 == 0 and n // 2 < GDN_STEPS else None


def fox_step(slot):
    n = slot - FOX_S
    return n // 2 if n >= 0 and n % 2 == 0 and n // 2 < FOX_STEPS else None


def gdn_place(step):
    half, n = divmod(step, HALF_STEPS)
    if n < 2 * UNIT_STEPS:
        return half, n // UNIT_STEPS, n % UNIT_STEPS
    return half, None, n - 2 * UNIT_STEPS


ACT_UNIT, ACT_CHAIN = 10, NCHUNK
DVE_UNIT, DVE_CHAIN = 11, 6
ACT_HALF, DVE_HALF = 2 * ACT_UNIT + ACT_CHAIN, 2 * DVE_UNIT + DVE_CHAIN


def chunk_of(n):
    return (0, True) if n == 0 else ((n + 1) // 2, n % 2 == 0)


def level_cols(ap, lv, odd):
    w = 1 << lv
    return ap.rearrange("p (a b) -> p a b", b=2 * w)[:, :, odd * w:(odd + 1) * w]


def gdn_base(half, unit, per_unit, per_half):
    return half * per_half + (2 if unit is None else unit) * per_unit


def dve_chain_base(chunk):
    return (0, 1, 3, 5)[chunk]


def slab_count(n, slot):
    return (n - slot) * (16 // RING) + 16


class Order:

    def __init__(self, eng, sem):
        self.eng, self.sem, self.base, self.n = eng, sem, 0, 0

    def then(self, ins, behind=0):
        self.n += 1
        ins.then_inc(self.sem, 1)
        self.eng.wait_ge(self.sem, self.base + self.n - behind)

    def enter(self, i, per):
        self.outer, self.per = self.base + self.n, per
        self.base, self.n = self.outer + i * per, 0

    def leave_body(self):
        assert self.n == self.per, (self.n, self.per)

    def leave(self, count):
        self.base, self.n = self.outer + count * self.per, 0


def build(nc, A, out):
    ctx = ExitStack()
    with ctx:
        base = 229376 - nc.sbuf_bytes_remaining
        base = (base + 63) // 64 * 64
        place = [base]

        def sb(name, shape, dt=F32, at=None):
            size = 4
            for s in shape[1:]:
                size *= s
            if at is None:
                at = place[0]
                place[0] += (size + 31) // 32 * 32
            return nc.alloc_sbuf_tensor_at(name, shape, dt, offset=at)

        K = 1024
        cst = sb("cst", [P, CONST.shape[1]])
        par = sb("par", [P, PO[-1]])
        act_hi = sb("act_hi", [P, DT, T], F32R)
        act_lo = sb("act_lo", [P, DT, T], F32R)
        w_f = sb("w_f", [P, RING, KS, NC])
        w_hi = sb("w_hi", [P, RING, KS, NC], F32R)
        w_lo = sb("w_lo", [P, RING, KS, NC], F32R)
        x_at = place[0]
        xres = sb("xres", [P, DT, T])
        eg_b = sb("eg_b", [P, 4, P], at=x_at)
        mt = sb("mt", [P, 4, P], at=x_at + 2 * K)
        lt = sb("lt", [P, 4, P], at=x_at + 4 * K)
        tinv = sb("tinv", [P, 4, P], at=x_at + 6 * K)
        tinv_t = sb("tinv_t", [P, 4, P], at=x_at + 8 * K)
        ys = sb("ys", [P, 4, P], at=x_at + 10 * K)
        state = sb("state", [P, 4, P], at=x_at + 12 * K)
        vnew = sb("vnew", [P, 4, P], at=x_at + 14 * K)
        rg = place[0]
        place[0] += 92 * K
        gdn_all = sb("gdn_all", [P, 3 * GDN_H, T], at=rg)
        gdn_q, gdn_k, gdn_v = (gdn_all[:, i * GDN_H:(i + 1) * GDN_H, :] for i in range(3))
        ob_hi = sb("ob_hi", [P, BR_T, T], F32R, at=rg + 8 * K)
        ob_lo = sb("ob_lo", [P, BR_T, T], F32R, at=rg + 16 * K)
        fox_all = sb("fox_all", [P, 3 * FOX_H, T], at=rg + 24 * K)
        fox_q, fox_k, fox_v = (fox_all[:, i * FOX_H:(i + 1) * FOX_H, :] for i in range(3))
        oa_hi = sb("oa_hi", [P, BR_T, T], F32R, at=rg + 24 * K)
        oa_lo = sb("oa_lo", [P, BR_T, T], F32R, at=rg + 32 * K)
        z_act = sb("z_act", [P, GDN_H, T], at=rg + 40 * K)
        cu_a = sb("cu_a", [P, CT, T], at=rg + 48 * K)
        conf = sb("conf", [P, CT, T], at=rg + 56 * K)
        oc_hi = sb("oc_hi", [P, BR_T, T], F32R, at=rg + 48 * K)
        oc_lo = sb("oc_lo", [P, BR_T, T], F32R, at=rg + 56 * K)
        y = sb("y", [P, DT, T], at=rg + 64 * K)
        attn_t = sb("attn_t", [P, 4, T], at=rg + 80 * K)
        w_t = sb("w_t", [P, 4, T], at=rg + 84 * K)
        gate = sb("gate", [P, NT, T], at=rg + 88 * K)
        x_tok = sb("x_tok", [P, TT, D], at=rg + 64 * K)
        junk = sb("junk", [P, D], at=x_at + 8 * K)
        par_rows = sb("par_rows", [P, len(PB), P], at=rg + 56 * K)
        nar_f = sb("nar_f", [P, DT, P], at=rg)
        nar_hi = sb("nar_hi", [P, DT, P], F32R, at=rg + 8 * K)
        nar_lo = sb("nar_lo", [P, DT, P], F32R, at=rg + 16 * K)
        mem_hi = sb("mem_hi", [P, DT, T], F32R, at=rg + 24 * K)
        mem_lo = sb("mem_lo", [P, DT, T], F32R, at=rg + 48 * K)
        m_tok = sb("m_tok", [P, D], at=rg + 80 * K)
        xr_tok = sb("xr_tok", [P, D], at=rg + 80 * K)
        xo_hi = sb("xo_hi", [P, XA_H, T], F32R, at=rg + 24 * K)
        xo_lo = sb("xo_lo", [P, XA_H, T], F32R, at=rg + 28 * K)
        xa_pt = sb("xa_pt", [P, XA_H, 2 * T], at=rg + 32 * K)
        xa_k = sb("xa_k", [P, XA_H, T], at=rg + 64 * K)
        xa_v = sb("xa_v", [P, XA_H, T], at=rg + 68 * K)
        xa_q = sb("xa_q", [P, XA_H, T], at=rg + 72 * K)
        xa_p = sb("xa_p", [P, XA_H, 2 * T], at=rg + 76 * K)
        HALF_T = 24
        g_hi = sb("g_hi", [P, HALF_T, T], F32R, at=rg)
        g_lo = sb("g_lo", [P, HALF_T, T], F32R, at=rg + 24 * K)
        ff_a = sb("ff_a", [P, NT, T], at=rg + 48 * K)
        ff_t = sb("ff_t", [P, NT, T], at=rg + 52 * K)
        out_tok = sb("out_tok", [P, TT, D], at=rg + 56 * K)
        split_t = sb("split_t", [P, 2, NT, P], at=x_at)
        split_w = sb("split_w", [P, 2, NT, T], at=rg)
        fx_s_at = place[0]
        fx_s = sb("fx_s", [P, 3 * P])
        fx_pt = sb("fx_pt", [P, 3 * P])
        tmp_w = sb("tmp_w", [P, T], at=fx_s_at)
        ms_w = sb("ms_w", [P, T])
        rs_w = sb("rs_w", [P, T])
        ms_t = sb("ms_t", [P, 4])
        rs_t = sb("rs_t", [P, 4])
        tmp_t = sb("tmp_t", [P, 4])
        ssum = sb("ssum", [P, 4])
        xa_m = sb("xa_m", [P, XA_H, TT])
        xa_ms = sb("xa_ms", [P, XA_H, TT])
        xa_rs = sb("xa_rs", [P, XA_H, TT])
        xa_tmp = sb("xa_tmp", [P, XA_H, TT])
        xa_sum = sb("xa_sum", [P, XA_H, 2])
        nar = sb("nar", [P, TT, 24])
        bias24 = sb("bias24", [P, 24])
        sp_v = sb("sp_v", [P, TT, 24])
        sp_a = sb("sp_a", [P, TT, 24])
        logf_n = sb("logf_n", [P, TT, 8])
        gdn_g = sb("gdn_g", [P, TT, 8])
        ln_beta = sb("ln_beta", [P, TT, 8])
        half_beta = sb("half_beta", [P, TT, 8])
        f_col = sb("f_col", [P, TT, 8])
        g_neg = sb("g_neg", [P, TT, 8])
        beta_eg = sb("beta_eg", [P, TT, 8])
        k_dec = sb("k_dec", [P, TT, 8])
        g_last = sb("g_last", [P, GDN_H, NCHUNK])
        fx_m = sb("fx_m", [P, 2])
        fx_sum = sb("fx_sum", [P, 2])
        qgain = sb("qgain", [P, 2])
        assert place[0] <= 229376, place[0]

        ps = [ctx.enter_context(nc.psum_tensor(f"ps{i}", [P, NT, T], F32)) for i in range(2)]
        bk = [ctx.enter_context(nc.psum_tensor(f"bk{i}", [P, 512], F32)) for i in range(4)]
        FA, FB, GA, GB = bk

        def sem(name):
            return ctx.enter_context(nc.semaphore(name))

        slab_loaded = [sem(f"slab_loaded{i}") for i in range(RING)]
        slab_hi, slab_lo, slab_used = sem("slab_hi"), sem("slab_lo"), sem("slab_used")
        group_read = sem("group_read")
        gates_read = sem("gates_read")
        ident_in, const_in, param_in = sem("ident_in"), sem("const_in"), sem("param_in")
        nar_clear, nar_in, bias_in = sem("nar_clear"), sem("nar_in"), sem("bias_in")
        x_in = [sem(f"x_in{t}") for t in range(TT)]
        mem_in = [sem(f"mem_in{t}") for t in range(TT)]
        xr_in = [sem(f"xr_in{t}") for t in range(TT)]
        out_st = sem("out_st")
        act_own, dve_own = sem("act_own"), sem("dve_own")
        pre_pe, pre_act, pre_dve = sem("pre_pe"), sem("pre_act"), sem("pre_dve")
        h_ready = sem("h_ready")
        silu_done = sem("silu_done")
        tanh_out = sem("tanh_out")
        y_added = sem("y_added")
        nm_pe, nm_act, nm_dve = sem("nm_pe"), sem("nm_act"), sem("nm_dve")
        cf_pe, cf_act, cf_dve = sem("cf_pe"), sem("cf_act"), sem("cf_dve")
        fx_pe, fx_act, fx_dve = sem("fx_pe"), sem("fx_act"), sem("fx_dve")
        gd_pe, gd_act, gd_dve = sem("gd_pe"), sem("gd_act"), sem("gd_dve")
        mm_pe, mm_act, mm_dve = sem("mm_pe"), sem("mm_act"), sem("mm_dve")
        xr_pe, xr_act = sem("xr_pe"), sem("xr_act")
        y_act, y_ready = sem("y_act"), sem("y_ready")
        mn_pe, mn_act, mn_dve = sem("mn_pe"), sem("mn_act"), sem("mn_dve")
        xa_pe, xa_act, xa_dve = sem("xa_pe"), sem("xa_act"), sem("xa_dve")
        ff_act, g_ready = sem("ff_act"), sem("g_ready")
        fin_pe, fin_act = sem("fin_pe"), sem("fin_act")

        def c(name, rows=slice(None)):
            a, b = CONST_AT[name]
            return cst[rows, a:b]

        def col(i):
            return par[:, i:i + 1]

        upto, ones, ident = c("upto"), c("ones"), c("ident")
        upto_ones = cst[:, CONST_AT["upto"][0]:CONST_AT["ones"][1]]
        zero_causal = cst[:, CONST_AT["zero"][0]:CONST_AT["not_causal"][1]]
        chunk_upto, chunk_after = c("chunk_upto"), c("chunk_after")

        def over(ap, n):
            return ap.unsqueeze(1).to_broadcast([ap.shape[0], n, ap.shape[1]])

        def spread(column, n=P):
            return column.to_broadcast([column.shape[0], n])

        def pick(i):
            o = CONST_AT["pick"][0]
            return cst[:, o + 15 - i:o + 31 - i]

        w_in, w_br, w_out = A["w_in"][0], A["w_branch"][0], A["w_out"][0]
        wq, wkv, wo = A["xattn_wq"][0], A["xattn_wkv"][0], A["xattn_wo"][0]
        w_up, w_down = A["ffn_w_up"][0], A["ffn_w_down"][0]

        block = ctx.enter_context(nc.Block())

        @block.sync
        def _(sp):
            sp.dma_start(x_tok[:, 0, :], A["x"][0, 0:P, :]).then_inc(x_in[0], 16)
            sp.dma_start(cst[:, 0:P], A["const"][:, 0:P]).then_inc(ident_in, 16)
            sp.dma_start(x_tok[:, 1, :], A["x"][0, P:T, :]).then_inc(x_in[1], 16)
            row = [0]

            def rows(blk, src):
                n = src.shape[0]
                sp.dma_start(par_rows[row[0]:row[0] + n, blk, :], src).then_inc(param_in, 16)
                row[0] += n

            for name in ("mix_norm_g", "mem_norm_g", "xattn_norm_g", "ffn_norm_g", "conf_dw_b", "conf_ln_g", "conf_ln_b"):
                v = A[name] if name == "mem_norm_g" else A[name][0]
                rows(0, v.rearrange("(r c) -> r c", c=P))
            for name in ("fox_q_norm_g", "fox_k_norm_g", "gdn_out_norm_g", "xattn_q_norm_g", "xattn_k_norm_g"):
                rows(0, A[name])
            row[0] = 0
            rows(1, A["gdn_conv_w"][0].rearrange("k (t c) -> (k t) c", c=P))
            row[0] = 0
            dw = A["conf_dw_w"][0].rearrange("k (t c) -> (k t) c", c=P)
            rows(2, dw[0:P, :])
            row[0] = 0
            rows(3, dw[P:CONF_TAPS * CT, :])
            row[0] = 0
            fw = A["ffn_conv_w"][0].rearrange("k (t c) -> (k t) c", c=P)
            rows(4, fw[0:2 * FT, :])
            row[0] = 0
            rows(5, fw[2 * FT:3 * FT, :])
            rows(5, A["ffn_conv_b"][0].rearrange("(r c) -> r c", c=P))
            def group(n0, w, k_slabs, g, c0, slot0=0, first=0):
                for j in range(k_slabs):
                    n, slot = n0 + j, (slot0 + j) % RING
                    if not isinstance(n, int) or n >= RING:
                        sp.wait_ge(slab_lo, n - (RING - 1))
                    r = (first + j) * KS * P
                    src = w[r:r + KS * P, bass.ds(g * NC + c0, NC)].rearrange("(a p) n -> p a n", p=P)
                    sp.dma_start(w_f[:, slot, :, :], src).then_inc(slab_loaded[slot], 16)

            group(0, w_in, RING, 0, CU_C)
            sp.dma_start(cst[:, P:], A["const"][:, P:]).then_inc(const_in, 16)
            for j, name in enumerate(("fox_fb", "gdn_dt_bias", "gdn_a_log")):
                sp.dma_start(bias24[:, 8 * j:8 * j + 8], A[name].to_broadcast([P, 8])).then_inc(bias_in, 16)
            w3 = w_in.rearrange("(a p) n -> p a n", p=P)
            sp.wait_ge(nar_clear, 1)
            sp.dma_start(nar_f[:, :, 0:8], w3[:, :, FF_C:FF_C + 8]).then_inc(nar_in, 16)
            sp.dma_start(nar_f[:, :, 8:24], w3[:, :, GAB_C:GAB_C + 16]).then_inc(nar_in, 16)
            group(RING, w_in, 8 - RING, 0, CU_C, first=RING)
            with sp.Fori(1, 4) as g:
                group(g * 8, w_in, 8, g, CU_C)
            for name, count, c0 in (("gdn", 6, GDN_C), ("fox", 6, FOX_C)):
                with sp.Fori(0, count) as g:
                    group(g * 8 + BASE[name], w_in, 8, g, c0)
            for n, name in ((2, "brC"), (0, "brA"), (1, "brB")):
                with sp.Fori(1, 5) as g:
                    group(g * 12 + (BASE[name] - 12), w_in, 8, g, GL_C + n * D - NC)
                    group(g * 12 + (BASE[name] - 4), w_br[n], 4, g, -NC)
                if name == "brC":
                    with sp.Fori(0, 2) as g:
                        group(g * 8 + BASE["z"], w_in, 8, g, Z_C)
            with sp.Fori(0, 4) as g:
                group(g * 8 + BASE["wout"], w_out, 8, g, 0)
            with sp.Fori(0, 2) as g:
                group(g * 8 + BASE["wkv"], wkv, 8, g, 0)
            group(BASE["wq"], wq, 8, 0, 0)
            for g in range(4):
                group(BASE["wo"] + 2 * g, wo, 2, g, 0, slot0=2 * g)
            for half, (a, pairs) in enumerate(((0, 6), (6, 5))):
                with sp.Fori(0, pairs) as g:
                    group(g * 16 + BASE[f"up{half}"], w_up, 8, g, a * NC)
                    group(g * 16 + (BASE[f"up{half}"] + 8), w_up, 8, g, a * NC + D_FF)
                per = 12 - 2 * half
                with sp.Fori(0, 2) as g2:
                    for k in range(2):
                        group(g2 * (2 * per) + (BASE[f"down{half}"] + k * per), w_down, per, g2 * 2, k * NC,
                              slot0=k * per, first=12 * half)
            for g in range(4):
                for t in range(TT):
                    sp.wait_ge(fin_act, 2 * g + t + 1)
                    cols = slice(g * NC, (g + 1) * NC)
                    sp.dma_start(out[0, t * P:(t + 1) * P, cols], out_tok[:, t, cols]).then_inc(out_st, 16)
            sp.wait_ge(out_st, 16 * 8)

        @block.tensor
        def _(pe):
            mm = nc.tensor.matmul
            transpose = nc.tensor.transpose

            def slab(n, slot, psum, hi, lo, k0, first, last):
                pe.wait_ge(slab_lo, n + 1)
                for kk in range(KS):
                    for j in range(NT):
                        wh = w_hi[:, slot, kk, j * P:(j + 1) * P]
                        wl = w_lo[:, slot, kk, j * P:(j + 1) * P]
                        o = psum[:, j, :]
                        mm(o, wh, hi[:, k0 + kk, :], start=first and kk == 0 and j % 2 == 0, stop=False, skip_group_check=True)
                        mm(o, wh, lo[:, k0 + kk, :], start=False, stop=False, skip_group_check=True)
                        i = mm(o, wl, hi[:, k0 + kk, :], start=False, stop=last and kk == KS - 1, skip_group_check=True)
                i.then_inc(slab_used, 1)

            def group(n0, buf, hi, lo, k_slabs, slot0=0, slots=None, ready=None):
                for j in range(k_slabs):
                    if ready is not None:
                        pe.wait_ge(ready[0], ready[1](j))
                    slab(n0 + j, (slot0 + j) % RING, ps[buf], hi, lo, KS * j, j == 0, j == k_slabs - 1)
                    if slots is not None:
                        slots(n0 + j)

            pe.wait_ge(ident_in, 16)
            pe.wait_ge(param_in, 16 * 18)
            for b, n in enumerate(PB):
                transpose(bk[b // 3][:, (b % 3) * P:(b % 3) * P + n], par_rows[0:n, b, :], ident[0:n, 0:n])\
                    .then_inc(pre_pe, 1)

            def x_batch(b):
                k, t = divmod(b, 2)
                pe.wait_ge(pre_dve, 3 + t)
                if b >= 4:
                    pe.wait_ge(pre_dve, b + 1)
                for j in range(4):
                    i = transpose(bk[b % 4][:, j * P:(j + 1) * P], x_tok[:, t, (4 * k + j) * P:(4 * k + j + 1) * P], ident)
                i.then_inc(pre_pe, 1)

            for b in range(4):
                x_batch(b)

            def narrow():
                pe.wait_ge(pre_dve, 13)
                for k in range(DT):
                    mm(FA[:, 0:T], nar_hi[:, k, :], act_hi[:, k, :], start=(k == 0), stop=False)
                    mm(FA[:, 0:T], nar_hi[:, k, :], act_lo[:, k, :], start=False, stop=False)
                    i = mm(FA[:, 0:T], nar_lo[:, k, :], act_hi[:, k, :], start=False, stop=(k == DT - 1))
                i.then_inc(pre_pe, 1)

            def narrow_by_token():
                pe.wait_ge(pre_dve, 14)
                for t in range(TT):
                    i = transpose(FB[:, t * 24:t * 24 + 24], tmp_w[0:24, t * P:(t + 1) * P], ident[0:24, 0:24])
                i.then_inc(pre_pe, 1)

            def token_sums():
                pe.wait_ge(const_in, 16)
                pe.wait_ge(pre_dve, 16)
                mm(FB[:, 0:8], upto, logf_n[:, 0, :], start=True, stop=True)
                mm(FB[:, 8:16], ones, logf_n[:, 0, :], start=True, stop=False)
                mm(FB[:, 8:16], upto, logf_n[:, 1, :], start=False, stop=True)
                for t in range(TT):
                    mm(FB[:, 16 + 8 * t:24 + 8 * t], chunk_upto, gdn_g[:, t, :], start=True, stop=True)
                    i = mm(FB[:, 32 + 8 * t:40 + 8 * t], chunk_after, gdn_g[:, t, :], start=True, stop=True)
                i.then_inc(pre_pe, 1)

            def head_norm(n, events, acc, banks, tiles, per_pair=1):
                _, a0, d0 = events
                nb = tiles // 4
                if n < nb:
                    pe.wait_ge(nm_act, a0 + n + 1)
                    for j in range(4):
                        i = mm(acc[0:16, 0:T], pick(4 * n + j), gate[:, j, :], start=(n == 0 and j == 0),
                               stop=(n == nb - 1 and j == 3))
                    i.then_inc(nm_pe, 1)
                    return
                for pr in (2 * (n - nb), 2 * (n - nb) + 1):
                    pe.wait_ge(nm_dve, d0 + 2 + (per_pair * (pr - 2) + 1 if pr >= 2 else 0))
                    for j in range(2):
                        i = mm(banks[pr % 2][:, j * T:(j + 1) * T], spread(ident[0:16, 2 * pr + j:2 * pr + j + 1]), rs_w[0:16, :],
                               start=(j == 0), stop=True, skip_group_check=True)
                    i.then_inc(nm_pe, 1)

            def fox_v_by_token(n):
                if n == 0:
                    pe.wait_ge(cf_dve, 3)
                    pe.wait_ge(nm_dve, NORM_OUT[2])
                for b in (2 * n, 2 * n + 1):
                    if b >= 2:
                        pe.wait_ge(fx_act, b - 1)
                    for j in range(4):
                        h, t = 2 * b + j // 2, j % 2
                        i = transpose((FA, FB)[b % 2][:, j * P:(j + 1) * P], fox_v[:, h, t * P:(t + 1) * P], ident)
                    i.then_inc(fx_pe, 1)

            def fox(step):
                h, s = divmod(step, 3)
                if s == 0:
                    pe.wait_ge(fx_act, 4 + 3 * h)
                    if h:
                        pe.wait_ge(fx_dve, 3 * h)
                    q, k = fox_q[:, h, :], fox_k[:, h, :]
                    mm(FA[:, 0:P], q[:, 0:P], k[:, 0:P], start=True, stop=False, skip_group_check=True)
                    mm(FA[:, P:3 * P], q[:, P:T], k, start=False, stop=False, skip_group_check=True)
                    f0, f1 = spread(logf_n[:, 0, h:h + 1]), spread(logf_n[:, 1, h:h + 1])
                    mm(FA[:, 0:P], f0, upto, start=False, stop=True, skip_group_check=True)
                    mm(FA[:, P:3 * P], f0, upto_ones, start=False, stop=False, skip_group_check=True)
                    i = mm(FA[:, 2 * P:3 * P], f1, upto, start=False, stop=True, skip_group_check=True)
                elif s == 1:
                    pe.wait_ge(fx_dve, 3 * h + 2)
                    for j in range(3):
                        i = transpose(FB[:, j * P:(j + 1) * P], fx_s[:, j * P:(j + 1) * P], ident)
                else:
                    pe.wait_ge(fx_act, 4 + 3 * h + 2)
                    v = fox_v[:, h, :]
                    mm(FA[:, 0:T], v[:, 0:P], fx_pt[:, 0:T], start=True, stop=False, skip_group_check=True)
                    i = mm(FA[:, P:T], v[:, P:T], fx_pt[:, T:3 * P], start=False, stop=True, skip_group_check=True)
                i.then_inc(fx_pe, 1)

            def gdn(step):
                half, unit, s = gdn_place(step)
                a0 = gdn_base(half, unit, ACT_UNIT, ACT_HALF)
                d0 = gdn_base(half, unit, DVE_UNIT, DVE_HALF)
                if unit is None:
                    gdn_chain(half, s, a0, d0)
                    return
                mats = [(2 * i + p, 4 * half + 2 * unit + i, p) for i in range(2) for p in range(2)]

                def tok(m, h, p):
                    return m[:, h, p * P:(p + 1) * P]

                def o(bank, m):
                    return bank[:, m * P:(m + 1) * P]

                if s == 0:
                    if step:
                        pe.wait_ge(gd_act, a0)
                        pe.wait_ge(gd_dve, d0)
                    else:
                        pe.wait_ge(nm_dve, NORM_FOX[2])
                    for m, h, p in mats:
                        mm(o(GA, m), spread(gdn_g[:, p, h:h + 1]), chunk_upto, start=(m == 0), stop=False, skip_group_check=True)
                    for m, h, p in mats:
                        i = mm(o(GB, m), tok(gdn_k, h, p), tok(gdn_q, h, p), start=True, stop=True)
                elif s == 1:
                    pe.wait_ge(gd_dve, d0 + 2)
                    for m, h, p in mats:
                        mm(o(GA, m), spread(ln_beta[:, p, h:h + 1]), ident, start=False, stop=True, skip_group_check=True)
                    for m, h, p in mats:
                        i = mm(o(GB, m), tok(gdn_k, h, p), tok(gdn_k, h, p), start=True, stop=True)
                elif s == 2:
                    pe.wait_ge(gd_dve, d0 + 4)
                    for m, h, p in mats:
                        i = transpose(o(GA, m), mt[:, m, :], ident)
                elif s < 13:
                    lv, second = (s - 1) // 2, (s - 3) % 2
                    if not second:
                        pe.wait_ge(gd_dve, d0 + 4 + lv)
                        for m, h, p in mats:
                            i = mm(o(GA, m), mt[:, m, :], tinv[:, m, :], start=True, stop=True)
                    else:
                        pe.wait_ge(gd_act, a0 + 3 + lv)
                        hp = P // 2
                        if lv < 5:
                            for m, h, p in mats:
                                mm(GB[:, m * hp:(m + 1) * hp], tinv_t[:, m, :], level_cols(ys[:, m, :], lv, 0), start=True, stop=True)
                        for m, h, p in mats:
                            i = mm(GA[:, m * hp:(m + 1) * hp], ys[:, m, :], level_cols(tinv_t[:, m, :], lv, 1), start=True, stop=True)
                elif s == 13:
                    pe.wait_ge(gd_dve, d0 + 10)
                    for m, h, p in mats:
                        transpose(o(GB, m), tok(gdn_k, h, p), ident)
                    for m, h, p in mats:
                        i = transpose(o(GA, m), tok(gdn_v, h, p), ident)
                else:
                    pe.wait_ge(gd_dve, d0 + 11)
                    pe.wait_ge(gd_act, a0 + 9)
                    for m, h, p in mats:
                        mm(o(GA, m), tinv_t[:, m, :], mt[:, m, :], start=True, stop=True)
                    for m, h, p in mats:
                        i = mm(o(GB, m), ys[:, m, :], tinv_t[:, m, :], start=True, stop=True)
                i.then_inc(gd_pe, 1)

            def gdn_chain(half, s, a0, d0):
                ch, second = chunk_of(s)
                p, r = ch // 2, slice((ch % 2) * CHUNK, (ch % 2 + 1) * CHUNK)
                tok = slice(ch * CHUNK, (ch + 1) * CHUNK)
                dc = d0 + dve_chain_base(ch)
                if not second:
                    pe.wait_ge(gd_dve, dc)
                    for i4 in range(4):
                        i = mm(GA[r, i4 * P:(i4 + 1) * P], w_t[:, i4, tok], state[:, i4, :], start=True, stop=True)
                    i.then_inc(gd_pe, 1)
                    return
                pe.wait_ge(gd_act, a0 + ch)
                pe.wait_ge(gd_dve, dc + 1 if ch else d0)
                for i4 in range(4):
                    h = 4 * half + i4
                    vn = vnew[r, i4, :] if ch else gdn_v[r, h, 0:P]
                    o = GB[:, i4 * CHUNK:(i4 + 1) * CHUNK]
                    if ch:
                        mm(o, state[:, i4, :], gdn_q[:, h, tok], start=True, stop=False)
                    i = mm(o, vn, attn_t[r, i4, tok], start=(ch == 0), stop=True)
                if ch < NCHUNK - 1:
                    for i4 in range(4):
                        h = 4 * half + i4
                        vn = vnew[r, i4, :] if ch else gdn_v[r, h, 0:P]
                        i = mm(GA[:, i4 * P:(i4 + 1) * P], gdn_k[r, h, p * P:(p + 1) * P], vn, start=True, stop=True)
                i.then_inc(gd_pe, 1)

            def conf_ln(n):
                if n == 0:
                    pe.wait_ge(nm_dve, NORM_OUT[2])
                    pe.wait_ge(cf_dve, 1)
                    for k in range(CT):
                        i = mm(FA[:, 0:T], ones, conf[:, k, :], start=(k == 0), stop=(k == CT - 1))
                else:
                    pe.wait_ge(cf_act, n)
                    for k in range(4):
                        i = mm(FA[:, T:2 * T], ones, gate[:, k, :], start=(n == 1 and k == 0), stop=(n == 2 and k == 3))
                i.then_inc(cf_pe, 1)

            def mem_batch(t, k):
                pe.wait_ge(mm_dve, 10 * t + 2 + 2 * k)
                for j in range(4):
                    i = transpose(FA[:, j * P:(j + 1) * P], m_tok[:, (4 * k + j) * P:(4 * k + j + 1) * P], ident)
                i.then_inc(mm_pe, 1)

            def xr_batch(t, k):
                b = 4 * t + k
                pe.wait_ge(xr_in[t], 16)
                if b >= 2:
                    pe.wait_ge(xr_act, b - 1)
                else:
                    pe.wait_ge(mm_dve, 20)
                for j in range(4):
                    i = transpose((FA, FB)[b % 2][:, j * P:(j + 1) * P], xr_tok[:, (4 * k + j) * P:(4 * k + j + 1) * P], ident)
                i.then_inc(xr_pe, 1)

            def slots(s):
                if s in X_S:
                    x_batch(4 + 2 * X_S.index(s))
                    x_batch(5 + 2 * X_S.index(s))
                if s == NARROW_S:
                    narrow()
                if s == NARROW_S + 1:
                    narrow_by_token()
                if s == TOKEN_S:
                    token_sums()
                if 0 <= s - GDN_N < 8:
                    head_norm(s - GDN_N, NORM_GDN, GA, (GA, GB), 16)
                if 0 <= s - FOX_N < 8:
                    head_norm(s - FOX_N, NORM_FOX, FA, (FA, FB), 16)
                if 0 <= s - CONF_S < 3:
                    conf_ln(s - CONF_S)
                if 0 <= s - FOX_V < 2:
                    fox_v_by_token(s - FOX_V)
                if fox_step(s) is not None:
                    fox(fox_step(s))
                if gdn_step(s) is not None:
                    gdn(gdn_step(s))
                if 0 <= s - GDN_OUT < 4:
                    if s == GDN_OUT:
                        pe.wait_ge(gd_act, 2 * ACT_HALF)
                        pe.wait_ge(gd_dve, 2 * DVE_HALF)
                    head_norm(s - GDN_OUT, NORM_OUT, GA, (GA, GB), 8, per_pair=2)
                for t in range(TT):
                    if s - MEM_S[t] in MEM_BATCH:
                        mem_batch(t, MEM_BATCH.index(s - MEM_S[t]))
                    if 0 <= s - XR_S[t] < 4:
                        xr_batch(t, s - XR_S[t])

            def even(name, i, hi, lo, k_slabs, slots=None, ready=None):
                r = READ[name] + i
                if r >= 2:
                    pe.wait_ge(group_read, r - 1)
                group(BASE[name] + i * k_slabs, i % 2, hi, lo, k_slabs, slot0=i * k_slabs, slots=slots, ready=ready)

            def branch(name, hi, lo, ready, last_gate):
                for g in range(4):
                    n0, gr = BASE[name] + 12 * g, GATES[name] + g
                    if g or last_gate:
                        pe.wait_ge(gates_read, gr)
                    else:
                        pe.wait_ge(group_read, READ[name] - 1)
                    group(n0, 0, act_hi, act_lo, 8, slots=slots)
                    pe.wait_ge(group_read, READ[name] + g)
                    if g == 0:
                        ready()
                    group(n0 + 8, 1, hi, lo, 4, slots=slots)

            for i in range(4):
                even("cu", i, act_hi, act_lo, 8, slots, (h_ready, lambda j: 2 * (j // 2) + 2) if i == 0 else None)
            with pe.Fori(0, 3) as g:
                for k in range(2):
                    pe.wait_ge(group_read, g * 2 + (READ["gdn"] + k - 1))
                    group(g * 16 + (BASE["gdn"] + 8 * k), k, act_hi, act_lo, 8)
            for i in range(6):
                even("fox", i, act_hi, act_lo, 8, slots)

            def conf_ready():
                pe.wait_ge(cf_dve, 8)

            def fox_ready():
                pe.wait_ge(fx_dve, 3 * FOX_H)

            def gdn_ready():
                pe.wait_ge(nm_dve, NORM_END[2])

            branch("brC", oc_hi, oc_lo, conf_ready, False)
            pe.wait_ge(gates_read, 4)
            for i in range(2):
                even("z", i, act_hi, act_lo, 8, slots)
            branch("brA", oa_hi, oa_lo, fox_ready, False)
            branch("brB", ob_hi, ob_lo, gdn_ready, True)

            pe.wait_ge(gates_read, 12)
            with pe.Fori(0, 2) as g:
                for k in range(2):
                    pe.wait_ge(group_read, g * 2 + (READ["wout"] + k - 1))
                    group(g * 16 + (BASE["wout"] + 8 * k), k, act_hi, act_lo, 8,
                          ready=(y_ready, lambda j: j // 2 + 1) if k == 0 else None)

            def x_norm_sums(m, b):
                pe.wait_ge(mn_act, 9 * m + b + 1)
                for j in range(4):
                    i = mm(FA[:, 0:T], ones, split_w[:, b % 2, j, :], start=(b == 0 and j == 0), stop=(b == 3 and j == 3))
                i.then_inc(mn_pe, 1)

            def xa_sums():
                pe.wait_ge(xa_act, 1)
                for j in range(4):
                    i = mm(FA[0:16, 0:T], pick(j), gate[:, j, :], start=(j == 0), stop=(j == 3))
                i.then_inc(xa_pe, 1)

            def xa_rms():
                pe.wait_ge(xa_dve, 2)
                for pr in range(2):
                    for j in range(2):
                        i = mm((FA, FB)[pr][:, j * T:(j + 1) * T], spread(ident[0:16, 2 * pr + j:2 * pr + j + 1]), rs_w[0:16, :],
                               start=(j == 0), stop=True, skip_group_check=True)
                    i.then_inc(xa_pe, 1)

            def late(s):
                if 0 <= s - NORM2 < 4:
                    x_norm_sums(0, s - NORM2)
                if s == XK_S + 1:
                    xa_sums()
                if s == XK_S + 3:
                    xa_rms()
                if s == XV_S:
                    pe.wait_ge(group_read, READ["wkv"] + 2)
                    for h in range(XA_H):
                        for t in range(TT):
                            i = transpose((GA, GB)[h // 2][:, (h % 2) * T + t * P:(h % 2) * T + (t + 1) * P],
                                          xa_v[:, h, t * P:(t + 1) * P], ident)
                    i.then_inc(xa_pe, 1)

            for i in range(2):
                even("wkv", i, mem_hi, mem_lo, 8, late)
            pe.wait_ge(mn_dve, 10)
            even("wq", 0, act_hi, act_lo, 8, late)
            pe.wait_ge(xa_dve, 4)
            pe.wait_ge(xa_act, 3)
            pe.wait_ge(group_read, READ["wq"] + 1)
            for h in range(XA_H):
                for t in range(TT):
                    i = mm(bk[h][:, t * T:(t + 1) * T], xa_q[:, h, t * P:(t + 1) * P], xa_k[:, h, :], start=True, stop=True)
                i.then_inc(xa_pe, 1)
                if h == 0:
                    pe.wait_ge(xa_act, 4)
                    for n in range(XA_H * TT):
                        i = mm(ps[1][:, 0, n:n + 1], gate[:, n // TT, (n % TT) * P:(n % TT + 1) * P], ones[:, 0:1], start=True, stop=True)
                    i.then_inc(xa_pe, 1)
            for h in range(XA_H):
                pe.wait_ge(xa_dve, 8 + h)
                for t in range(TT):
                    for m in range(2):
                        i = transpose(bk[h][:, m * T + t * P:m * T + (t + 1) * P], xa_p[:, h, t * T + m * P:t * T + (m + 1) * P], ident)
                i.then_inc(xa_pe, 1)
            for h in range(XA_H):
                pe.wait_ge(xa_act, 10 + h)
                for m in range(2):
                    i = mm(bk[h][:, 0:T], xa_v[:, h, m * P:(m + 1) * P], xa_pt[:, h, m * T:(m + 1) * T], start=(m == 0), stop=(m == 1))
                i.then_inc(xa_pe, 1)
            pe.wait_ge(xa_dve, 15)
            for i in range(4):
                pe.wait_ge(group_read, READ["wo"] + i - (i > 0))
                group(BASE["wo"] + 2 * i, i % 2, xo_hi, xo_lo, 2, slot0=2 * i)
                if i:
                    x_norm_sums(1, i - 1)
            x_norm_sums(1, 3)

            done = 0
            for half, pairs in enumerate((6, 5)):
                r = READ[f"up{half}"]
                with pe.Fori(0, pairs) as g:
                    for k in range(2):
                        pe.wait_ge(group_read, g * 2 + (r + k - 1))
                        group(g * 16 + (BASE[f"up{half}"] + 8 * k), k, act_hi, act_lo, 8,
                              ready=(mn_dve, lambda j: 10 + X_LOW[j // 2]) if half + k == 0 else None)
                per, r = 12 - 2 * half, READ[f"down{half}"]
                with pe.Fori(0, 2 - half) as g:
                    for k in range(2):
                        pe.wait_ge(group_read, g * 2 + (r + k - 1))
                        group(g * (2 * per) + (BASE[f"down{half}"] + k * per), k, g_hi, g_lo, per, slot0=k * per,
                              ready=(g_ready, lambda j: done + j // 2 + 1))
                done += pairs

            def by_token(g):
                pe.wait_ge(group_read, READ["down1"] + g + 1)
                for t in range(TT):
                    b = 2 * g + t
                    if b >= 4:
                        pe.wait_ge(fin_act, b - 3)
                    for j in range(4):
                        i = transpose(bk[b % 4][:, j * P:(j + 1) * P], xres[:, 4 * g + j, t * P:(t + 1) * P], ident)
                    i.then_inc(fin_pe, 1)

            for g in (2, 3):
                pe.wait_ge(group_read, r + g - 1)
                group(BASE["down1"] + g * per, g % 2, g_hi, g_lo, per, slot0=g * per,
                      slots=lambda s: by_token(OUT_S.index(s)) if s in OUT_S else None)
            by_token(3)

        @block.scalar
        def _(act):
            own = Order(act, act_own)
            op = nc.scalar.activation

            def split(n, slot):
                act.wait_ge(slab_loaded[slot], slab_count(n, slot))
                if not isinstance(n, int) or n >= RING:
                    act.wait_ge(slab_used, n - (RING - 1))
                op(w_hi[:, slot, :, :], w_f[:, slot, :, :], ACT.Copy).then_inc(slab_hi, 1)

            def rsqrt(dst, src):
                own.then(op(dst, src, ACT.Ln))
                return op(dst, dst, ACT.Exp, scale=-0.5)

            for t in range(TT):
                act.wait_ge(x_in[t], 16)
                if t:
                    act.wait_ge(pre_act, 1)
                op(junk[:, :], x_tok[:, t, :], ACT.Square, accum_out=ssum[:, t:t + 1]).then_inc(pre_act, 1)
            act.wait_ge(pre_dve, 2)
            rsqrt(rs_t[:, 0:TT], ms_t[:, 0:TT]).then_inc(pre_act, 1)
            for n in range(LEAD):
                split(n, n)

            def x_batch(b):
                k, t = divmod(b, 2)
                act.wait_ge(pre_dve, 5 + b)
                op(act_hi[:, 4 * k:4 * k + 4, t * P:(t + 1) * P], split_t[:, b % 2, :, :], ACT.Copy).then_inc(pre_act, 1)

            for b in range(4):
                x_batch(b)

            def narrow_split():
                act.wait_ge(nar_in, 32)
                op(nar_hi[:, :, :], nar_f[:, :, :], ACT.Copy).then_inc(pre_act, 1)

            def softplus():
                act.wait_ge(bias_in, 48)
                own.then(op(bias24[:, 16:24], bias24[:, 16:24], ACT.Exp))
                act.wait_ge(pre_dve, 15)
                own.then(op(sp_a[:, :, :], sp_v[:, :, :], ACT.Abs))
                own.then(op(sp_a[:, :, :], sp_a[:, :, :], ACT.Exp, scale=-1.0))
                op(sp_a[:, :, :], sp_a[:, :, :], ACT.Ln, bias=1.0).then_inc(pre_act, 1)

            def token_exps():
                act.wait_ge(pre_dve, 16)
                op(half_beta[:, :, :], ln_beta[:, :, :], ACT.Exp).then_inc(pre_act, 1)
                act.wait_ge(pre_dve, 17)
                op(k_dec[:, :, :], FB[:, 32:48], ACT.Exp)
                op(beta_eg[:, :, :], beta_eg[:, :, :], ACT.Exp).then_inc(pre_act, 1)

            def head_norm(n, events, region, tiles):
                p0, a0, d0 = events
                nb = tiles // 4
                if n < nb:
                    if n:
                        act.wait_ge(nm_pe, p0 + n)
                    op(gate[:, :, :], region[:, 4 * n:4 * n + 4, :], ACT.Square).then_inc(nm_act, 1)
                elif n == nb:
                    act.wait_ge(nm_dve, d0 + 1)
                    rsqrt(rs_w[0:16, :], ms_w[0:16, :]).then_inc(nm_act, 1)

            def conf_ln(n):
                half = (slice(None), slice(0, 4) if n < 5 else slice(4, 8), slice(None))
                if n in (1, 2):
                    act.wait_ge(cf_dve, 2)
                    if n == 1:
                        act.wait_ge(nm_dve, NORM_OUT[2])
                    if n == 2:
                        act.wait_ge(cf_pe, 2)
                    op(gate[:, :, :], conf[:, 4 * n - 4:4 * n, :], ACT.Square).then_inc(cf_act, 1)
                elif n == 3:
                    act.wait_ge(cf_dve, 3)
                    rsqrt(rs_w[:, :], ms_w[:, :]).then_inc(cf_act, 1)
                if n == 5:
                    act.wait_ge(cf_dve, 5)
                    op(oc_hi[:, 0:4, :], conf[:, 0:4, :], ACT.Copy, scale=0.5).then_inc(cf_act, 1)
                if n in (4, 5):
                    act.wait_ge(cf_dve, 4)
                    for k in range(4 * n - 16, 4 * n - 12):
                        i = op(conf[:, k, :], conf[:, k, :], ACT.Identity, scale=col(C_LNG + k), bias=col(C_LNB + k))
                    i.then_inc(cf_act, 1)
                if n in (4, 6):
                    act.wait_ge(cf_act, 4 if n == 4 else 7)
                    op(gate[:, :, :], conf[half], ACT.Tanh, scale=0.5).then_inc(cf_act, 1)
                if n == 7:
                    act.wait_ge(cf_dve, 7)
                    op(oc_hi[half], conf[half], ACT.Copy, scale=0.5).then_inc(cf_act, 1)

            def fox_v_by_token(n):
                for b in (2 * n, 2 * n + 1):
                    act.wait_ge(fx_pe, b + 1)
                    op(fox_v[:, 2 * b:2 * b + 2, :], (FA, FB)[b % 2][:, :], ACT.Copy).then_inc(fx_act, 1)

            def fox(step):
                h, s = divmod(step, 3)
                if s == 0:
                    act.wait_ge(fx_dve, 3 * h + 1)
                    op(fx_s[:, 0:P], fx_s[:, 0:P], ACT.Exp, bias=fx_m[:, 0:1], accum_out=fx_sum[:, 0:1])
                    op(fx_s[:, P:3 * P], fx_s[:, P:3 * P], ACT.Exp, bias=fx_m[:, 1:2], accum_out=fx_sum[:, 1:2]).then_inc(fx_act, 1)
                elif s == 1:
                    act.wait_ge(fx_pe, 4 + 3 * h + 2)
                    op(fx_pt[:, :], FB[:, 0:3 * P], ACT.Copy).then_inc(fx_act, 1)
                else:
                    act.wait_ge(fx_pe, 4 + 3 * h + 3)
                    op(oa_hi[:, h, :], FA[:, 0:T], ACT.Copy).then_inc(fx_act, 1)

            def gdn(step):
                half, unit, s = gdn_place(step)
                if chunk_of(s)[1] if unit is None else s in (0, 3, 5, 7, 9, 11, 13, 14):
                    act.wait_ge(gd_pe, step + 1)
                d0 = gdn_base(half, unit, DVE_UNIT, DVE_HALF)
                if unit is None:
                    ch, second = chunk_of(s)
                    if second:
                        op(gdn_q[:, 4 * half:4 * half + 4, ch * CHUNK:(ch + 1) * CHUNK], GB[:, 0:4 * CHUNK], ACT.Copy).then_inc(gd_act, 1)
                    return
                h0 = 4 * half + 2 * unit
                if s == 0:
                    op(eg_b[:, :, :], GA[:, :], ACT.Exp).then_inc(gd_act, 1)
                    act.wait_ge(gd_dve, d0 + 1)
                    op(mt[:, :, :], mt[:, :, :], ACT.Exp).then_inc(gd_act, 1)
                elif s == 1:
                    act.wait_ge(gd_dve, d0 + 3)
                    op(lt[:, :, :], lt[:, :, :], ACT.Exp).then_inc(gd_act, 1)
                elif s in (3, 5, 7, 9, 11):
                    op(ys[:, :, :], GA[:, :], ACT.Copy).then_inc(gd_act, 1)
                elif s == 13:
                    for m in range(4):
                        h, p = h0 + m // 2, m % 2
                        op(ys[:, m, :], GB[:, m * P:(m + 1) * P], ACT.Copy, scale=beta_eg[:, p, h:h + 1])
                        i = op(gdn_k[:, h, p * P:(p + 1) * P], GB[:, m * P:(m + 1) * P], ACT.Copy, scale=k_dec[:, p, h:h + 1])
                    i.then_inc(gd_act, 1)
                elif s == 14:
                    op(gdn_v[:, h0:h0 + 2, :], GA[:, :], ACT.Copy)
                    op(w_t[:, 2 * unit:2 * unit + 2, :], GB[:, :], ACT.Copy).then_inc(gd_act, 1)

            def gdn_out(n):
                head_norm(n, NORM_OUT, gdn_q, 8)
                if n >= 2:
                    for pr in (2 * (n - 2), 2 * (n - 2) + 1):
                        act.wait_ge(nm_dve, NORM_OUT[2] + 2 + 2 * pr + 1)
                        op(ob_hi[:, 2 * pr:2 * pr + 2, :], gdn_q[:, 2 * pr:2 * pr + 2, :], ACT.Copy).then_inc(nm_act, 1)

            def slots(s):
                if s in X_S:
                    x_batch(4 + 2 * X_S.index(s))
                    x_batch(5 + 2 * X_S.index(s))
                if s == X_S[1] + 1:
                    narrow_split()
                if s == NARROW_S + 1:
                    softplus()
                if s == TOKEN_S:
                    token_exps()
                if 0 <= s - GDN_N < 8:
                    if s == GDN_N:
                        act.wait_ge(silu_done, 6)
                    head_norm(s - GDN_N, NORM_GDN, gdn_all, 16)
                if 0 <= s - FOX_N < 8:
                    head_norm(s - FOX_N, NORM_FOX, fox_all, 16)
                if 0 <= s - CONF_S < 8:
                    conf_ln(s - CONF_S)
                if 0 <= s - FOX_V < 2:
                    fox_v_by_token(s - FOX_V)
                if fox_step(s) is not None:
                    fox(fox_step(s))
                if gdn_step(s) is not None:
                    gdn(gdn_step(s))
                if 0 <= s - GDN_OUT < 4:
                    if s == GDN_OUT:
                        act.wait_ge(y_added, 4)
                    gdn_out(s - GDN_OUT)
                for t in range(TT):
                    if s == MEM_LOAD[t]:
                        act.wait_ge(gd_pe, GDN_STEPS)
                        if t:
                            act.wait_ge(mm_pe, 4)
                        act.dma_start(m_tok[:, :], A["mem"][0, t * P:(t + 1) * P, :]).then_inc(mem_in[t], 16)
                    if s == MEM_S[t]:
                        act.wait_ge(mem_in[t], 16)
                        op(junk[:, :], m_tok[:, :], ACT.Square, accum_out=ssum[:, 2 + t:3 + t]).then_inc(mm_act, 1)
                    if s == MEM_S[t] + 1:
                        act.wait_ge(mm_dve, 10 * t + 1)
                        rsqrt(rs_t[:, 2 + t:3 + t], ms_t[:, 2 + t:3 + t]).then_inc(mm_act, 1)
                    if s - MEM_S[t] in MEM_BATCH:
                        k = MEM_BATCH.index(s - MEM_S[t])
                        act.wait_ge(mm_dve, 10 * t + 3 + 2 * k)
                        op(mem_hi[:, 4 * k:4 * k + 4, t * P:(t + 1) * P], split_t[:, 0, :, :], ACT.Copy).then_inc(mm_act, 1)
                    if s == XR_LOAD[t]:
                        act.wait_ge(mm_pe, 8)
                        if t:
                            act.wait_ge(xr_pe, 4)
                        act.dma_start(xr_tok[:, :], A["x"][0, t * P:(t + 1) * P, :]).then_inc(xr_in[t], 16)
                    if 0 <= s - XR_S[t] < 4:
                        k = s - XR_S[t]
                        act.wait_ge(xr_pe, 4 * t + k + 1)
                        act.wait_ge(mm_dve, 20)
                        op(xres[:, 4 * k:4 * k + 4, t * P:(t + 1) * P], (FA, FB)[k % 2][:, :], ACT.Copy).then_inc(xr_act, 1)
                if 0 <= s - Y_SPLIT < 4:
                    g = s - Y_SPLIT
                    act.wait_ge(slab_used, Y_SPLIT)
                    act.wait_ge(y_added, 4 + g + 1)
                    op(act_hi[:, 4 * g:4 * g + 4, :], y[:, 4 * g:4 * g + 4, :], ACT.Copy, scale=0.5).then_inc(y_act, 1)

            def step(s, part):
                if s + LEAD < SLABS:
                    split(s + LEAD, (s + LEAD) % RING)
                part(s)

            def loop_split(n, j):
                split(n + (j + LEAD), (j + LEAD) % RING)

            for i in range(4):
                for j in range(8):
                    step(BASE["cu"] + 8 * i + j, slots)
                if i >= 2:
                    if i == 3:
                        act.wait_ge(group_read, 3)
                    act.wait_ge(slab_used, BASE["cu"] + 8 * i + 8)
                    op(gate[:, :, :], ps[i % 2][:, :, :], ACT.Tanh, scale=0.5).then_inc(tanh_out, 1)
            def silu(i):
                act.wait_ge(group_read, READ["gdn"] + i + 1)
                op(gate[:, :, :], gdn_all[:, 4 * i:4 * i + 4, :], ACT.Tanh, scale=0.5).then_inc(tanh_out, 1)

            for i in range(6):
                n0 = BASE["gdn"] + 8 * i
                for j in range(8):
                    step(n0 + j, slots)
                    if j == SILU_J and i:
                        silu(i - 1)
                act.wait_ge(slab_used, n0 + 8)
                for j in range(NT):
                    k = 4 * i + j
                    e = op(gdn_all[:, k, :], ps[i % 2][:, j, :], ACT.Copy, scale=col(C_GDN + (GDN_TAPS - 1) * 24 + k))
                e.then_inc(tanh_out, 1)
            for i in range(6):
                for j in range(8):
                    step(BASE["fox"] + 8 * i + j, slots)
                    if i == 0 and j == SILU_J:
                        silu(5)
                act.wait_ge(slab_used, BASE["fox"] + 8 * i + 8)
                act.wait_ge(group_read, READ["fox"] + i)
                op(fox_all[:, 4 * i:4 * i + 4, :], ps[i % 2][:, :, :], ACT.Copy).then_inc(group_read, 1)

            def branch(name):
                for g in range(4):
                    n0 = BASE[name] + 12 * g
                    for j in range(8):
                        step(n0 + j, slots)
                    act.wait_ge(slab_used, n0 + 8)
                    if name == "brC":
                        act.wait_ge(cf_dve, 8)
                        act.wait_ge(group_read, READ[name] + g)
                    elif name == "brA" and g == 0:
                        act.wait_ge(group_read, READ[name])
                    else:
                        act.wait_ge(y_added, GATES[name] - 4 + g)
                    op(gate[:, :, :], ps[0][:, :, :], ACT.Tanh, scale=0.5).then_inc(gates_read, 1)
                    for j in range(8, 12):
                        step(n0 + j, slots)

            branch("brC")
            for i in range(2):
                for j in range(8):
                    step(BASE["z"] + 8 * i + j, slots)
                act.wait_ge(slab_used, BASE["z"] + 8 * i + 8)
                act.wait_ge(group_read, READ["z"] + i)
                op(gate[:, :, :], ps[i % 2][:, :, :], ACT.Tanh, scale=0.5).then_inc(tanh_out, 1)
            branch("brA")
            branch("brB")
            with act.Fori(0, 4) as g:
                for j in range(8):
                    loop_split(g * 8 + BASE["wout"], j)

            def x_norm(m, n):
                if n < 4:
                    if n >= 2:
                        act.wait_ge(mn_pe, 4 * m + n - 1)
                    op(split_w[:, n % 2, :, :], xres[:, 4 * n:4 * n + 4, :], ACT.Square).then_inc(mn_act, 1)
                elif n == 4:
                    act.wait_ge(mn_dve, 10 * m + 1)
                    rsqrt(rs_w[:, :], ms_w[:, :]).then_inc(mn_act, 1)
                else:
                    b = n - 5
                    act.wait_ge(mn_dve, 10 * m + X_SCALED[b])
                    op(act_hi[:, 4 * b:4 * b + 4, :], split_w[:, b % 2, :, :], ACT.Copy).then_inc(mn_act, 1)

            def late(s):
                if 0 <= s - NORM2 < 9:
                    if s == NORM2:
                        act.wait_ge(group_read, READ["wkv"])
                        act.wait_ge(slab_used, BASE["wkv"])
                    x_norm(0, s - NORM2)
                if s == XK_S:
                    act.wait_ge(mn_dve, 10)
                    act.wait_ge(group_read, READ["wkv"] + 1)
                    op(gate[:, :, :], xa_k[:, :, :], ACT.Square).then_inc(xa_act, 1)
                if s == XK_S + 2:
                    act.wait_ge(xa_dve, 1)
                    rsqrt(rs_w[0:16, :], ms_w[0:16, :]).then_inc(xa_act, 1)
                if s == XV_S:
                    act.wait_ge(xa_pe, 4)
                    for i in range(2):
                        e = op(xa_v[:, 2 * i:2 * i + 2, :], (GA, GB)[i][:, :], ACT.Copy)
                    e.then_inc(xa_act, 1)

            for s in range(BASE["wkv"], BASE["wo"]):
                step(s, late)
            act.wait_ge(group_read, READ["wq"] + 1)
            op(gate[:, :, :], ps[0][:, :, :], ACT.Square).then_inc(xa_act, 1)
            act.wait_ge(xa_dve, 5)
            rsqrt(xa_rs[:, :, :], xa_ms[:, :, :]).then_inc(xa_act, 1)
            act.wait_ge(xa_dve, 7)
            for h in range(XA_H):
                for t in range(TT):
                    e = op(xa_p[:, h, t * T:(t + 1) * T], bk[h][:, t * T:(t + 1) * T], ACT.Exp, bias=xa_m[:, h, t:t + 1],
                           scale=xa_rs[:, h, t:t + 1], accum_out=xa_sum[:, h, t:t + 1])
                e.then_inc(xa_act, 1)
            for h in range(XA_H):
                act.wait_ge(xa_pe, 10 + h)
                op(xa_pt[:, h, :], bk[h][:, :], ACT.Copy).then_inc(xa_act, 1)
            for h in range(XA_H):
                act.wait_ge(xa_pe, 14 + h)
                op(xo_hi[:, h, :], bk[h][:, 0:T], ACT.Copy).then_inc(xa_act, 1)
            for i in range(4):
                for j in range(2):
                    step(BASE["wo"] + 2 * i + j, lambda s: None)
                if i:
                    act.wait_ge(group_read, READ["wo"] + i)
                    x_norm(1, i - 1)
            act.wait_ge(group_read, READ["up0"])
            for n in range(3, 9):
                x_norm(1, n)

            def conv_col(tap, half, g, j):
                a = C_FFW + tap * FT if tap is not None else C_FFB
                return par[:, bass.ds(g * NT + (a + 24 * half + j), 1)]

            done = 0
            for half, pairs in enumerate((6, 5)):
                r = READ[f"up{half}"]
                with act.Fori(0, pairs) as g:
                    n0 = g * 16 + BASE[f"up{half}"]
                    for j in range(8):
                        loop_split(n0, j)
                    act.wait_ge(slab_used, n0 + 8)
                    for j in range(NT):
                        e = op(ff_a[:, j, :], ps[0][:, j, :], ACT.Identity, scale=conv_col(2, half, g, j), bias=conv_col(None, half, g, j))
                    e.then_inc(ff_act, 1)
                    for j in range(8):
                        loop_split(n0 + 8, j)
                        if j == 1:
                            act.wait_ge(group_read, g * 2 + (r + 1))
                            op(ff_t[:, :, :], ff_a[:, :, :], ACT.Tanh, scale=0.5).then_inc(ff_act, 1)
                    act.wait_ge(group_read, g * 2 + (r + 2))
                    op(g_hi[:, bass.ds(g * NT, NT), :], ff_a[:, :, :], ACT.Copy).then_inc(ff_act, 1)
                done += pairs
                per = 12 - 2 * half
                n0 = BASE[f"down{half}"]
                with act.Fori(0, 2 - half) as g:
                    for j in range(2 * per):
                        loop_split(g * (2 * per) + n0, j)

            def by_token(g):
                for t in range(TT):
                    act.wait_ge(fin_pe, 2 * g + t + 1)
                    op(out_tok[:, t, 4 * g * P:4 * (g + 1) * P], bk[(2 * g + t) % 4][:, :], ACT.Copy).then_inc(fin_act, 1)

            for s in range(BASE["down1"] + 2 * per, SLABS):
                step(s, lambda s: by_token(OUT_S.index(s)) if s in OUT_S else None)
            by_token(3)

        @block.vector
        def _(dve):
            own = Order(dve, dve_own)
            v = nc.vector
            stt, tsc, tt_ = v.scalar_tensor_tensor, v.tensor_scalar, v.tensor_tensor

            def split(n, slot):
                dve.wait_ge(slab_hi, n + 1)
                tt_(w_lo[:, slot, :, :], w_f[:, slot, :, :], w_hi[:, slot, :, :].bitcast(F32), ALU.subtract).then_inc(slab_lo, 1)

            def newton(r, ms, tmp):
                own.then(tt_(tmp, r, r, ALU.mult))
                own.then(stt(tmp, tmp, -0.5, ms, ALU.mult, ALU.mult))
                return stt(r, tmp, 1.5, r, ALU.add, ALU.mult)

            v.memset(nar_f[:, :, 24:P], 0.0).then_inc(nar_clear, 1)
            dve.wait_ge(pre_pe, 6)
            for b, n in enumerate(PB):
                e = v.tensor_copy(par[:, PO[b]:PO[b] + n], bk[b // 3][:, (b % 3) * P:(b % 3) * P + n])
            e.then_inc(pre_dve, 1)
            dve.wait_ge(pre_act, 2)
            tsc(ms_t[:, 0:TT], ssum[:, 0:TT], 1.0 / D, EPS, ALU.mult, ALU.add).then_inc(pre_dve, 1)
            dve.wait_ge(pre_act, 3)
            own.then(newton(rs_t[:, 0:TT], ms_t[:, 0:TT], tmp_t[:, 0:TT]))
            for t in range(TT):
                tsc(x_tok[:, t, :], x_tok[:, t, :], rs_t[:, t:t + 1], None, ALU.mult).then_inc(pre_dve, 1)

            def x_batches(b0):
                k = b0 // 2
                gains = par[:, G_MIX + 4 * k:G_MIX + 4 * k + 4].unsqueeze(2).to_broadcast([P, 4, P])
                for b in (b0, b0 + 1):
                    dve.wait_ge(pre_pe, 7 + b)
                    if b >= 2:
                        dve.wait_ge(h_ready, b - 1)
                    tt_(split_t[:, b % 2, :, :], bk[b % 4][:, :].rearrange("p (a b) -> p a b", a=4), gains, ALU.mult).then_inc(pre_dve, 1)
                for b in (b0, b0 + 1):
                    dve.wait_ge(pre_act, 4 + b)
                    cols = (slice(None), slice(4 * k, 4 * k + 4), slice((b % 2) * P, (b % 2 + 1) * P))
                    tt_(act_lo[cols], split_t[:, b % 2, :, :], act_hi[cols].bitcast(F32), ALU.subtract).then_inc(h_ready, 1)

            dve.wait_ge(pre_dve, 1)
            x_batches(0)
            for n in range(LEAD):
                split(n, n)
                if n == 0:
                    x_batches(2)

            def narrow_split():
                dve.wait_ge(pre_act, 12)
                tt_(nar_lo[:, :, :], nar_f[:, :, :], nar_hi[:, :, :].bitcast(F32), ALU.subtract).then_inc(pre_dve, 1)

            def narrow():
                dve.wait_ge(pre_pe, 15)
                v.tensor_copy(tmp_w[0:24, :], FA[0:24, 0:T]).then_inc(pre_dve, 1)

            def decay_logs():
                dve.wait_ge(pre_pe, 16)
                own.then(v.tensor_copy(nar[:, :, :], FB[:, 0:48].rearrange("p (a b) -> p a b", a=TT)))
                dve.wait_ge(bias_in, 48)
                stt(sp_v[:, :, 0:8], nar[:, :, 0:8], -1.0, over(bias24[:, 0:8], TT), ALU.mult, ALU.subtract)
                tt_(sp_v[:, :, 8:16], nar[:, :, 8:16], over(bias24[:, 8:16], TT), ALU.add)
                tsc(sp_v[:, :, 16:24], nar[:, :, 16:24], -1.0, None, ALU.mult).then_inc(pre_dve, 1)
                dve.wait_ge(pre_dve, 15)
                dve.wait_ge(pre_act, 13)
                own.then(stt(sp_v[:, :, :], sp_v[:, :, :], 0.0, sp_a[:, :, :], ALU.max, ALU.add))
                v.tensor_copy(logf_n[:, :, :], sp_v[:, :, 0:8])
                stt(gdn_g[:, :, :], sp_v[:, :, 8:16], -1.0, over(bias24[:, 16:24], TT), ALU.mult, ALU.mult)
                tsc(ln_beta[:, :, :], sp_v[:, :, 16:24], -1.0, None, ALU.mult).then_inc(pre_dve, 1)

            def token_columns():
                dve.wait_ge(pre_dve, 16)
                dve.wait_ge(pre_pe, 17)

                def by(a):
                    return FB[:, a:a + 16].rearrange("p (a b) -> p a b", a=TT)
                tsc(f_col[:, :, :], by(0), -1.0, None, ALU.mult)
                tsc(g_neg[:, :, :], by(16), -1.0, None, ALU.mult)
                tt_(beta_eg[:, :, :], by(16), ln_beta[:, :, :], ALU.add).then_inc(pre_dve, 1)
                dve.wait_ge(pre_act, 14)
                tsc(half_beta[:, :, :], half_beta[:, :, :], 0.5, None, ALU.mult)
                tsc(qgain[:, 0:1], col(G_FQ), HD ** -0.5, None, ALU.mult)
                tsc(qgain[:, 1:2], col(G_XQ), HD ** -0.5, None, ALU.mult).then_inc(pre_dve, 1)
                dve.wait_ge(pre_dve, 18)

            def head_norm(n, events, region, tiles, acc, banks, scale, gain, after=None):
                p0, a0, d0 = events
                nb = tiles // 4
                if n == nb - 1:
                    dve.wait_ge(nm_pe, p0 + nb)
                    tsc(ms_w[0:16, :], acc[0:16, 0:T], scale, EPS, ALU.mult, ALU.add).then_inc(nm_dve, 1)
                if n < nb:
                    return
                if n == nb:
                    dve.wait_ge(nm_act, a0 + nb + 1)
                    newton(rs_w[0:16, :], ms_w[0:16, :], tmp_w[0:16, :]).then_inc(nm_dve, 1)
                for pr in (2 * (n - nb), 2 * (n - nb) + 1):
                    dve.wait_ge(nm_pe, p0 + nb + pr + 1)
                    two = region[:, 2 * pr:2 * pr + 2, :]
                    e = stt(two, two, gain(2 * pr), banks[pr % 2][:, :].rearrange("p (a b) -> p a b", a=2), ALU.mult, ALU.mult)
                    if after is None:
                        e.then_inc(nm_dve, 1)
                    else:
                        after(pr, own.then(e))

            def conf_taps(s):
                total = CT * CONF_TAPS
                n, slots = CONV_SLOTS.index(s), len(CONV_SLOTS)
                for i in range(total * n // slots, total * (n + 1) // slots):
                    pair, j = divmod(i, 2 * CONF_TAPS)
                    k, back = 2 * pair + j % 2, j // 2
                    w = col(C_CONF + (CONF_TAPS - 1 - back) * CT + k)
                    if back == 0:
                        own.then(tsc(conf[:, k, :], cu_a[:, k, :], w, col(C_DWB + k), ALU.mult, ALU.add), behind=1)
                    else:
                        e = stt(conf[:, k, back:T], cu_a[:, k, 0:T - back], w, conf[:, k, back:T], ALU.mult, ALU.add)
                        if i == total - 1:
                            e.then_inc(cf_dve, 1)
                        else:
                            own.then(e, behind=1)

            def conf_ln(n):
                if n == 0:
                    dve.wait_ge(cf_pe, 1)
                    mean = FA[:, 0:T].unsqueeze(1).to_broadcast([P, 4, T])
                    for k in range(2):
                        e = stt(conf[:, 4 * k:4 * k + 4, :], mean, -1.0 / CONV_CH, conf[:, 4 * k:4 * k + 4, :], ALU.mult, ALU.add)
                    e.then_inc(cf_dve, 1)
                elif n == 2:
                    dve.wait_ge(cf_pe, 3)
                    tsc(ms_w[:, :], FA[:, T:2 * T], 1.0 / CONV_CH, LN_EPS, ALU.mult, ALU.add).then_inc(cf_dve, 1)
                elif n == 3:
                    dve.wait_ge(cf_act, 3)
                    own.then(newton(rs_w[:, :], ms_w[:, :], tmp_w[:, :]))
                    rs = over(rs_w[:, :], 4)
                    for k in range(2):
                        e = tt_(conf[:, 4 * k:4 * k + 4, :], conf[:, 4 * k:4 * k + 4, :], rs, ALU.mult)
                    e.then_inc(cf_dve, 1)
                elif n >= 4:
                    hf = (n - 4) // 2
                    half = (slice(None), slice(4 * hf, 4 * hf + 4), slice(None))
                    if n % 2 == 0:
                        dve.wait_ge(cf_act, 5 + 3 * hf)
                        stt(conf[half], gate[:, :, :], 1.0, conf[half], ALU.add, ALU.mult).then_inc(cf_dve, 1)
                    else:
                        dve.wait_ge(cf_act, 6 + 3 * hf)
                        stt(oc_lo[half], conf[half], 0.5, oc_hi[half].bitcast(F32), ALU.mult, ALU.subtract).then_inc(cf_dve, 1)

            def fox(step):
                h, s = divmod(step, 3)
                if s == 0:
                    dve.wait_ge(fx_pe, 4 + 3 * h + 1)
                    stt(fx_s[:, 0:P], FA[:, 0:P], f_col[:, 0, h:h + 1], c("not_causal"), ALU.add, ALU.add)
                    own.then(stt(fx_s[:, P:3 * P], FA[:, P:3 * P], f_col[:, 1, h:h + 1], zero_causal, ALU.add, ALU.add))
                    v.reduce_max(fx_m[:, 0:1], fx_s[:, 0:P], AX.X)
                    own.then(v.reduce_max(fx_m[:, 1:2], fx_s[:, P:3 * P], AX.X))
                    tsc(fx_m[:, :], fx_m[:, :], -1.0, None, ALU.mult).then_inc(fx_dve, 1)
                    dve.wait_ge(fx_act, 4 + 3 * h + 1)
                    own.then(v.reciprocal(fx_sum[:, :], fx_sum[:, :]))
                    tsc(fx_s[:, 0:P], fx_s[:, 0:P], fx_sum[:, 0:1], None, ALU.mult)
                    tsc(fx_s[:, P:3 * P], fx_s[:, P:3 * P], fx_sum[:, 1:2], None, ALU.mult).then_inc(fx_dve, 1)
                elif s == 2:
                    dve.wait_ge(fx_act, 4 + 3 * h + 3)
                    tt_(oa_lo[:, h, :], FA[:, 0:T], oa_hi[:, h, :].bitcast(F32), ALU.subtract).then_inc(fx_dve, 1)

            def gdn(step):
                half, unit, s = gdn_place(step)
                a0 = gdn_base(half, unit, ACT_UNIT, ACT_HALF)
                if unit is None:
                    gdn_chain(half, step, s)
                    return
                h0 = 4 * half + 2 * unit
                mats = [(2 * i + p, h0 + i, p) for i in range(2) for p in range(2)]

                def o(bank, m):
                    return bank[:, m * P:(m + 1) * P]

                def by4(bank):
                    return bank[:, :].rearrange("p (a b) -> p a b", a=4)

                def level(lv):
                    return tt_(mt[:, :, :], lt[:, :, :], over(c(f"level{lv}"), 4), ALU.mult)

                if s in (0, 1, 2, 4, 6, 8, 10, 12, 13):
                    dve.wait_ge(gd_pe, step + 1)
                if step == 0:
                    dve.wait_ge(nm_dve, NORM_FOX[2])
                if s == 0:
                    dve.wait_ge(gd_act, a0 + 1)
                    for m, h, p in mats:
                        e = stt(mt[:, m, :], o(GA, m), g_neg[:, p, h:h + 1], c("not_before"), ALU.add, ALU.add)
                    e.then_inc(gd_dve, 1)
                    dve.wait_ge(gd_act, a0 + 2)
                    tt_(attn_t[:, 2 * unit:2 * unit + 2, :], GB[:, :].rearrange("p (a b) -> p a b", a=2),
                        mt[:, :, :].rearrange("p (a c) b -> p a (c b)", a=2), ALU.mult)
                    eg = eg_b[:, :, :].rearrange("p (a c) b -> p a (c b)", a=2)
                    v.tensor_copy(g_last[:, h0:h0 + 2, :], eg[:, :, CHUNK - 1::CHUNK])
                    tt_(gdn_q[:, h0:h0 + 2, :], gdn_q[:, h0:h0 + 2, :], eg, ALU.mult).then_inc(gd_dve, 1)
                elif s == 1:
                    for m, h, p in mats:
                        e = stt(lt[:, m, :], o(GA, m), g_neg[:, p, h:h + 1], c("not_strict"), ALU.add, ALU.add)
                    e.then_inc(gd_dve, 1)
                    dve.wait_ge(gd_act, a0 + 3)
                    own.then(tt_(lt[:, :, :], by4(GB), lt[:, :, :], ALU.mult))
                    own.then(level(0))
                    tt_(tinv_t[:, :, :], over(ident, 4), mt[:, :, :], ALU.subtract).then_inc(gd_dve, 1)
                elif s == 2:
                    tt_(tinv[:, :, :], over(ident, 4), by4(GA), ALU.subtract)
                    level(1).then_inc(gd_dve, 1)
                elif s in (4, 6, 8, 10, 12):
                    lv = (s - 2) // 2

                    def less(mat, bank, odd):
                        cols = level_cols(mat[:, :, :].rearrange("p m c -> p (m c)"), lv, odd)
                        return tt_(cols, cols, bank[:, 0:2 * P].rearrange("p (a b) -> p a b", b=1 << lv), ALU.subtract)

                    if lv < 5:
                        less(tinv, GB, 0)
                        less(tinv_t, GA, 1)
                        level(lv + 1).then_inc(gd_dve, 1)
                    else:
                        less(tinv_t, GA, 1).then_inc(gd_dve, 1)
                elif s == 13:
                    for m, h, p in mats:
                        e = tsc(mt[:, m, :], o(GA, m), half_beta[:, p, h:h + 1], None, ALU.mult)
                    e.then_inc(gd_dve, 1)

            def gdn_chain(half, step, s):
                ch, second = chunk_of(s)
                p, r = ch // 2, slice((ch % 2) * CHUNK, (ch % 2 + 1) * CHUNK)
                dve.wait_ge(gd_pe, step + 1)
                if not second:
                    tt_(vnew[r, :, :], gdn_v[r, 4 * half:4 * half + 4, p * P:(p + 1) * P],
                        GA[r, :].rearrange("p (a b) -> p a b", a=4), ALU.subtract).then_inc(gd_dve, 1)
                elif ch == 0:
                    v.tensor_copy(state[:, :, :], GA[:, :].rearrange("p (a b) -> p a b", a=4)).then_inc(gd_dve, 1)
                elif ch < NCHUNK - 1:
                    for i4 in range(4):
                        e = stt(state[:, i4, :], state[:, i4, :], g_last[:, 4 * half + i4, ch:ch + 1], GA[:, i4 * P:(i4 + 1) * P], ALU.mult, ALU.add)
                    e.then_inc(gd_dve, 1)

            def gdn_gate(pr, _):
                two = (slice(None), slice(2 * pr, 2 * pr + 2), slice(None))
                stt(gdn_q[two], gdn_q[two], 0.5, z_act[two], ALU.mult, ALU.mult).then_inc(nm_dve, 1)
                dve.wait_ge(nm_act, NORM_OUT[1] + 3 + pr + 1)
                tt_(ob_lo[two], gdn_q[two], ob_hi[two].bitcast(F32), ALU.subtract).then_inc(nm_dve, 1)

            def mem_scale(t):
                cl = slice(2 + t, 3 + t)
                dve.wait_ge(mm_act, 6 * t + 2)
                own.then(newton(rs_t[:, cl], ms_t[:, cl], tmp_t[:, cl]))
                tsc(m_tok[:, :], m_tok[:, :], rs_t[:, cl], None, ALU.mult).then_inc(mm_dve, 1)

            def mem_batch(t, k):
                dve.wait_ge(mm_pe, 4 * t + k + 1)
                gains = par[:, G_MEM + 4 * k:G_MEM + 4 * k + 4].unsqueeze(2).to_broadcast([P, 4, P])
                tt_(split_t[:, 0, :, :], FA[:, :].rearrange("p (a b) -> p a b", a=4), gains, ALU.mult).then_inc(mm_dve, 1)
                dve.wait_ge(mm_act, 6 * t + 3 + k)
                cols = (slice(None), slice(4 * k, 4 * k + 4), slice(t * P, (t + 1) * P))
                tt_(mem_lo[cols], split_t[:, 0, :, :], mem_hi[cols].bitcast(F32), ALU.subtract).then_inc(mm_dve, 1)

            def slots(s):
                if s in X_S:
                    x_batches(4 + 2 * X_S.index(s))
                if s == X_S[1] + 1:
                    narrow_split()
                if s == NARROW_S:
                    narrow()
                if s == NARROW_S + 1:
                    decay_logs()
                if s == TOKEN_S:
                    token_columns()
                if s in CONV_SLOTS:
                    conf_taps(s)
                if 0 <= s - GDN_N < 8:
                    head_norm(s - GDN_N, NORM_GDN, gdn_all, 16, GA, (GA, GB), 0.25, lambda i: 0.5 * HD ** -0.5 if i < 8 else 0.5)
                if 0 <= s - FOX_N < 8:
                    head_norm(s - FOX_N, NORM_FOX, fox_all, 16, FA, (FA, FB), 1.0 / HD, lambda i: qgain[:, 0:1] if i < 8 else col(G_FK))
                if 0 <= s - CONF_S < 8:
                    conf_ln(s - CONF_S)
                if fox_step(s) is not None:
                    fox(fox_step(s))
                if gdn_step(s) is not None:
                    gdn(gdn_step(s))
                if 0 <= s - GDN_OUT < 4:
                    head_norm(s - GDN_OUT, NORM_OUT, gdn_q, 8, GA, (GA, GB), 1.0 / HD, lambda i: col(G_GO), after=gdn_gate)
                for t in range(TT):
                    if s == MEM_S[t]:
                        dve.wait_ge(mm_act, 6 * t + 1)
                        tsc(ms_t[:, 2 + t:3 + t], ssum[:, 2 + t:3 + t], 1.0 / D, EPS, ALU.mult, ALU.add).then_inc(mm_dve, 1)
                    if s == MEM_S[t] + 1:
                        mem_scale(t)
                    if s - MEM_S[t] in MEM_BATCH:
                        mem_batch(t, MEM_BATCH.index(s - MEM_S[t]))
                if 0 <= s - Y_SPLIT < 4:
                    g = s - Y_SPLIT
                    if g == 3:
                        return
                    y_split(g)

            def y_split(g):
                dve.wait_ge(y_act, g + 1)
                four = (slice(None), slice(4 * g, 4 * g + 4), slice(None))
                stt(act_lo[four], y[four], 0.5, act_hi[four].bitcast(F32), ALU.mult, ALU.subtract).then_inc(y_ready, 1)

            def step(s, part):
                if s + LEAD < SLABS:
                    split(s + LEAD, (s + LEAD) % RING)
                part(s)

            def loop_split(n, j):
                split(n + (j + LEAD), (j + LEAD) % RING)

            for i in range(4):
                n0 = BASE["cu"] + 8 * i
                for j in range(8):
                    step(n0 + j, slots)
                dve.wait_ge(slab_used, n0 + 8)
                if i < 2:
                    tsc(cu_a[:, 4 * i:4 * i + 4, :], ps[i % 2][:, :, :], 0.5, None, ALU.mult).then_inc(group_read, 1)
                else:
                    dve.wait_ge(tanh_out, i - 1)
                    a = cu_a[:, 4 * i - 8:4 * i - 4, :]
                    stt(a, gate[:, :, :], 1.0, a, ALU.add, ALU.mult).then_inc(group_read, 1)
            dve.wait_ge(group_read, 4)

            def silu(i):
                dve.wait_ge(tanh_out, 2 + 2 * i + 2)
                four = gdn_all[:, 4 * i:4 * i + 4, :]
                stt(four, gate[:, :, :], 1.0, four, ALU.add, ALU.mult).then_inc(silu_done, 1)
                dve.wait_ge(silu_done, i + 1)

            def conv_silu(i, j):
                if j == 0:
                    dve.wait_ge(tanh_out, 2 + 2 * i + 1)
                if j < GDN_TAPS - 1:
                    back = j + 1
                    for n in range(NT):
                        k = 4 * i + n
                        w = col(C_GDN + (GDN_TAPS - 1 - back) * 24 + k)
                        o = gdn_all[:, k, back:T]
                        e = stt(o, ps[i % 2][:, n, 0:T - back], w, o, ALU.mult, ALU.add)
                    if back < GDN_TAPS - 1:
                        own.then(e)
                    else:
                        e.then_inc(group_read, 1)
                if j == SILU_J:
                    silu(i)

            for i in range(6):
                n0 = BASE["gdn"] + 8 * i
                for j in range(8):
                    step(n0 + j, slots)
                    if i:
                        conv_silu(i - 1, j)
            for i in range(6):
                n0 = BASE["fox"] + 8 * i
                for j in range(8):
                    step(n0 + j, slots)
                    if i == 0:
                        conv_silu(5, j)

            def branch(name):
                for g in range(4):
                    n0 = BASE[name] + 12 * g
                    for j in range(12):
                        step(n0 + j, slots)
                    dve.wait_ge(slab_used, n0 + 12)
                    dve.wait_ge(gates_read, GATES[name] + g + 1)
                    four = y[:, 4 * g:4 * g + 4, :]
                    o = four if name == "brC" else gate[:, :, :]
                    stt(o, gate[:, :, :], 1.0, ps[1][:, :, :], ALU.add, ALU.mult).then_inc(group_read, 1)
                    if name != "brC":
                        dve.wait_ge(group_read, READ[name] + g + 1)
                        tt_(four, four, gate[:, :, :], ALU.add).then_inc(y_added, 1)

            branch("brC")
            for i in range(2):
                n0 = BASE["z"] + 8 * i
                for j in range(8):
                    step(n0 + j, slots)
                if i == 0:
                    dve.wait_ge(fx_pe, 4 + FOX_STEPS)
                dve.wait_ge(tanh_out, 14 + i + 1)
                stt(z_act[:, 4 * i:4 * i + 4, :], gate[:, :, :], 1.0, ps[i % 2][:, :, :], ALU.add, ALU.mult).then_inc(group_read, 1)
            branch("brA")
            branch("brB")
            y_split(3)
            dve.wait_ge(xr_act, 8)
            with dve.Fori(0, 2) as g:
                for k in range(2):
                    n0 = g * 16 + (BASE["wout"] + 8 * k)
                    for j in range(8):
                        loop_split(n0, j)
                    dve.wait_ge(slab_used, n0 + 8)
                    four = xres[:, bass.ds(g * 8 + 4 * k, 4), :]
                    tt_(four, four, ps[k][:, :, :], ALU.add).then_inc(group_read, 1)

            def x_norm(m, n, gain):
                if n == 3:
                    dve.wait_ge(mn_pe, 4 * m + 4)
                    tsc(ms_w[:, :], FA[:, 0:T], 1.0 / D, EPS, ALU.mult, ALU.add).then_inc(mn_dve, 1)
                elif n == 4:
                    dve.wait_ge(mn_act, 9 * m + 5)
                    newton(rs_w[:, :], ms_w[:, :], tmp_w[:, :]).then_inc(mn_dve, 1)
                    dve.wait_ge(mn_dve, 10 * m + 2)
                if 5 <= n < 9:
                    scaled(m, n - 5, gain)
                if 6 <= n < 10:
                    low(m, n - 6)

            def scaled(m, b, gain):
                if b >= 2:
                    dve.wait_ge(mn_dve, 10 * m + X_LOW[b - 2])
                for j in range(4):
                    e = stt(split_w[:, b % 2, j, :], xres[:, 4 * b + j, :], col(gain + 4 * b + j), rs_w[:, :], ALU.mult, ALU.mult)
                e.then_inc(mn_dve, 1)

            def low(m, b):
                dve.wait_ge(mn_act, 9 * m + 6 + b)
                four = (slice(None), slice(4 * b, 4 * b + 4), slice(None))
                tt_(act_lo[four], split_w[:, b % 2, :, :], act_hi[four].bitcast(F32), ALU.subtract).then_inc(mn_dve, 1)

            def late(s):
                if 0 <= s - NORM2 < 10:
                    x_norm(0, s - NORM2, G_XA)
                if s == XK_S + 1:
                    dve.wait_ge(xa_pe, 1)
                    tsc(ms_w[0:16, :], FA[0:16, 0:T], 1.0 / HD, EPS, ALU.mult, ALU.add).then_inc(xa_dve, 1)
                if s == XK_S + 2:
                    dve.wait_ge(xa_act, 2)
                    newton(rs_w[0:16, :], ms_w[0:16, :], tmp_w[0:16, :]).then_inc(xa_dve, 1)
                if s == XK_S + 3:
                    for pr in range(2):
                        dve.wait_ge(xa_pe, 2 + pr)
                        two = xa_k[:, 2 * pr:2 * pr + 2, :]
                        stt(two, two, col(G_XK), (FA, FB)[pr][:, :].rearrange("p (a b) -> p a b", a=2), ALU.mult, ALU.mult).then_inc(xa_dve, 1)

            for i, dst in enumerate((xa_k, xa_v)):
                n0 = BASE["wkv"] + 8 * i
                for j in range(8):
                    step(n0 + j, late)
                dve.wait_ge(slab_used, n0 + 8)
                v.tensor_copy(dst[:, :, :], ps[i % 2][:, :, :]).then_inc(group_read, 1)
            for j in range(8):
                step(BASE["wq"] + j, late)
            dve.wait_ge(slab_used, BASE["wq"] + 8)
            tsc(xa_q[:, :, :], ps[0][:, :, :], qgain[:, 1:2], None, ALU.mult).then_inc(group_read, 1)
            dve.wait_ge(xa_pe, 6)
            tsc(xa_ms[:, :, :], ps[1][:, 0, 0:XA_H * TT].rearrange("p (a b) -> p a b", a=XA_H), 1.0 / HD, EPS, ALU.mult, ALU.add)\
                .then_inc(xa_dve, 1)
            for h in range(XA_H):
                if h:
                    dve.wait_ge(xa_pe, 6 + h)
                own.then(v.reduce_max(xa_m[:, h, :], bk[h][:, :].rearrange("p (a b) -> p a b", a=TT), AX.X))
            dve.wait_ge(xa_act, 5)
            newton(xa_rs[:, :, :], xa_ms[:, :, :], xa_tmp[:, :, :]).then_inc(xa_dve, 1)
            dve.wait_ge(xa_dve, 6)
            stt(xa_m[:, :, :], xa_m[:, :, :], -1.0, xa_rs[:, :, :], ALU.mult, ALU.mult).then_inc(xa_dve, 1)
            for h in range(XA_H):
                dve.wait_ge(xa_act, 6 + h)
                own.then(v.reciprocal(xa_sum[:, h, :], xa_sum[:, h, :]))
                for t in range(TT):
                    pt = xa_p[:, h, t * T:(t + 1) * T]
                    e = tsc(pt, pt, xa_sum[:, h, t:t + 1], None, ALU.mult)
                e.then_inc(xa_dve, 1)
            for h in range(XA_H):
                dve.wait_ge(xa_act, 14 + h)
                tt_(xo_lo[:, h, :], bk[h][:, 0:T], xo_hi[:, h, :].bitcast(F32), ALU.subtract).then_inc(xa_dve, 1)
            for i in range(4):
                n0 = BASE["wo"] + 2 * i
                for j in range(2):
                    step(n0 + j, lambda s: None)
                dve.wait_ge(slab_used, n0 + 2)
                four = xres[:, 4 * i:4 * i + 4, :]
                tt_(four, four, ps[i % 2][:, :, :], ALU.add).then_inc(group_read, 1)
            dve.wait_ge(group_read, READ["up0"])
            for n in range(3, 10):
                x_norm(1, n, G_FFN)

            def conv_col(tap, half, g, j):
                return par[:, bass.ds(g * NT + (C_FFW + tap * FT + 24 * half + j), 1)]

            done = 0
            for half, pairs in enumerate((6, 5)):
                with dve.Fori(0, pairs) as g:
                    own.enter(g, 2)
                    n0 = g * 16 + BASE[f"up{half}"]
                    for j in range(8):
                        loop_split(n0, j)
                    dve.wait_ge(ff_act, g * 3 + (3 * done + 1))
                    for back in range(1, FFN_TAPS):
                        for j in range(NT):
                            o = ff_a[:, j, back:T]
                            e = stt(o, ps[0][:, j, 0:T - back], conv_col(FFN_TAPS - 1 - back, half, g, j), o, ALU.mult, ALU.add)
                        if back == 1:
                            own.then(e)
                    e.then_inc(group_read, 1)
                    for j in range(8):
                        loop_split(n0 + 8, j)
                        if j == 2:
                            dve.wait_ge(ff_act, g * 3 + (3 * done + 2))
                            own.then(stt(ff_a[:, :, :], ff_t[:, :, :], 1.0, ff_a[:, :, :], ALU.add, ALU.mult))
                    dve.wait_ge(slab_used, n0 + 16)
                    stt(ff_a[:, :, :], ff_a[:, :, :], 0.5, ps[1][:, :, :], ALU.mult, ALU.mult).then_inc(group_read, 1)
                    dve.wait_ge(ff_act, g * 3 + (3 * done + 3))
                    tt_(g_lo[:, bass.ds(g * NT, NT), :], ff_a[:, :, :], g_hi[:, bass.ds(g * NT, NT), :].bitcast(F32), ALU.subtract)\
                        .then_inc(g_ready, 1)
                    own.leave_body()
                own.leave(pairs)
                done += pairs
                per = 12 - 2 * half
                n0 = BASE[f"down{half}"]

                def add(n_end, k, at):
                    dve.wait_ge(slab_used, n_end)
                    four = xres[:, at, :]
                    tt_(four, four, ps[k][:, :, :], ALU.add).then_inc(group_read, 1)

                with dve.Fori(0, 2 - half) as g:
                    for k in range(2):
                        for j in range(per):
                            loop_split(g * (2 * per) + n0, k * per + j)
                        add(g * (2 * per) + (n0 + (k + 1) * per), k, bass.ds(g * 8 + 4 * k, 4))
                if half:
                    for k in range(2):
                        for j in range(per):
                            if 2 * per + k * per + j + LEAD < 4 * per:
                                loop_split(n0 + 2 * per, k * per + j)
                        add(n0 + (3 + k) * per, k, slice(8 + 4 * k, 12 + 4 * k))


_INS = ["x", "mem", "mix_norm_g", "w_in", "fox_fb", "fox_q_norm_g", "fox_k_norm_g", "gdn_conv_w", "gdn_a_log",
        "gdn_dt_bias", "gdn_out_norm_g", "conf_dw_w", "conf_dw_b", "conf_ln_g", "conf_ln_b", "w_branch", "w_out",
        "mem_norm_g", "xattn_norm_g", "xattn_wq", "xattn_wkv", "xattn_q_norm_g", "xattn_k_norm_g", "xattn_wo",
        "ffn_norm_g", "ffn_w_up", "ffn_conv_w", "ffn_conv_b", "ffn_w_down"]


def kernel(**inputs):
    import concourse.bacc as bacc
    from concourse.bass_utils import run_bass_kernel_spmd

    nc = bacc.Bacc("TRN2", target_bir_lowering=False, num_devices=1)
    arrays, aps = {}, {}
    for name in _INS + ["const"]:
        a = np.ascontiguousarray(CONST if name == "const" else inputs[name])
        arrays[f"in_{name}"] = a
        aps[name] = nc.dram_tensor(f"in_{name}", a.shape, mybir.dt.from_np(a.dtype), kind="ExternalInput").ap()
    out = nc.dram_tensor("out_x", (1, T, D), F32, kind="ExternalOutput").ap()
    build(nc, aps, out)
    r = run_bass_kernel_spmd(nc, [arrays], core_ids=[0])
    return r.results[0]["out_x"]
```
